# Optimizing a Trainium2 kernel written in Bass

```python
import jax, jax.numpy as jnp
from jax import lax
import numpy as np
import math

D_MODEL = 2048
BATCH = 1
SEQ = 256
DEPTH = 2

CHUNK = 64
Q_BLOCK = 128
N_A = DEPTH // 2
N_B = DEPTH - N_A
PLE_DIM = 256
RMS_EPS = 1e-6
NEG_INF = -1e30

SB_HEAD_DIM = 128
SB_HEADS = D_MODEL // SB_HEAD_DIM
SB_WIDTH = SB_HEADS * SB_HEAD_DIM

QK_NOPE_DIM = 128
QK_ROPE_DIM = 64
V_HEAD_DIM = 128
MLA_HEADS = D_MODEL // V_HEAD_DIM
Q_LORA_RANK = D_MODEL // 4
KV_LORA_RANK = D_MODEL // 4
MLA_WIDTH = MLA_HEADS * V_HEAD_DIM
QK_HEAD_DIM = QK_NOPE_DIM + QK_ROPE_DIM
ROPE_THETA = 10000.0


def rms_norm(x, g):
    xf = x.astype(jnp.float32)
    y = xf * lax.rsqrt(jnp.mean(xf * xf, axis=-1, keepdims=True) + RMS_EPS)
    return (y * g.astype(jnp.float32)).astype(x.dtype)

def rope_tables(seq_len):
    inv = 1.0 / (ROPE_THETA ** (jnp.arange(0, QK_ROPE_DIM, 2, dtype=jnp.float32) / QK_ROPE_DIM))
    ang = jnp.arange(seq_len, dtype=jnp.float32)[:, None] * inv[None, :]
    return jnp.cos(ang), jnp.sin(ang)

def apply_rope(t, cos, sin):
    tf = t.astype(jnp.float32)
    t1, t2 = jnp.split(tf, 2, axis=-1)
    return jnp.concatenate([t1 * cos - t2 * sin, t1 * sin + t2 * cos], axis=-1).astype(t.dtype)

def to_blocks(t):
    b, s = t.shape[:2]
    t = t.reshape((b, s // Q_BLOCK, Q_BLOCK) + t.shape[2:])
    return jnp.moveaxis(t, 1, 0)

def from_blocks(t):
    t = jnp.moveaxis(t, 0, 1)
    return t.reshape((t.shape[0], t.shape[1] * t.shape[2]) + t.shape[3:])

def stick_breaking_attention(q, k, v):
    s_len, dh = q.shape[1], q.shape[-1]
    scale = dh ** -0.5
    kpos = jnp.arange(s_len)

    def one_block(args):
        i, qi = args
        qpos = i * Q_BLOCK + jnp.arange(Q_BLOCK)
        z = jnp.einsum('bqhd,bkhd->bhqk', qi, k, preferred_element_type=jnp.float32) * scale
        strict = kpos[None, :] < qpos[:, None]
        log_keep = jnp.where(strict, jax.nn.log_sigmoid(-z), 0.0)
        later = lax.cumsum(log_keep, axis=3, reverse=True) - log_keep
        w = jnp.where(strict, jnp.exp(jax.nn.log_sigmoid(z) + later), 0.0)
        return jnp.einsum('bhqk,bkhd->bqhd', w.astype(v.dtype), v)

    out = lax.map(one_block, (jnp.arange(s_len // Q_BLOCK), to_blocks(q)))
    return from_blocks(out)

def mla_attention(q_nope, q_rope, k_nope, k_rope, v):
    s_len = q_nope.shape[1]
    scale = QK_HEAD_DIM ** -0.5
    kchunk = jnp.arange(s_len) // CHUNK

    def one_block(args):
        i, qn, qr = args
        qchunk = (i * Q_BLOCK + jnp.arange(Q_BLOCK)) // CHUNK
        s = (jnp.einsum('bqhd,bkhd->bhqk', qn, k_nope, preferred_element_type=jnp.float32)
             + jnp.einsum('bqhr,bkr->bhqk', qr, k_rope, preferred_element_type=jnp.float32)) * scale
        s = jnp.where(kchunk[None, :] <= qchunk[:, None], s, NEG_INF)
        prob = jax.nn.softmax(s, axis=-1)
        return jnp.einsum('bhqk,bkhd->bqhd', prob.astype(v.dtype), v)

    out = lax.map(one_block, (jnp.arange(s_len // Q_BLOCK), to_blocks(q_nope), to_blocks(q_rope)))
    return from_blocks(out)

def mixer_a(h, w_in, w_out):
    b, s, _ = h.shape
    q, k, v, g = jnp.split(h @ w_in, 4, axis=-1)
    heads = lambda t: t.reshape(b, s, SB_HEADS, SB_HEAD_DIM)
    o = stick_breaking_attention(heads(q), heads(k), heads(v)).reshape(b, s, SB_WIDTH)
    return (o * jax.nn.silu(g)) @ w_out

def shared_kv(x, kv_norm, w_dkv, kv_latent_norm, w_uk, w_uv, cos, sin):
    b, s, _ = x.shape
    ckv, k_rope = jnp.split(rms_norm(x, kv_norm) @ w_dkv, [KV_LORA_RANK], axis=-1)
    ckv = rms_norm(ckv, kv_latent_norm)
    k_nope = (ckv @ w_uk).reshape(b, s, MLA_HEADS, QK_NOPE_DIM)
    v = (ckv @ w_uv).reshape(b, s, MLA_HEADS, V_HEAD_DIM)
    k_rope = apply_rope(k_rope, cos, sin)
    return k_nope, k_rope, v

def mixer_b(h, kv, w_in, q_latent_norm, w_uq, w_out, cos, sin):
    b, s, _ = h.shape
    k_nope, k_rope, v = kv
    cq, g = jnp.split(h @ w_in, [Q_LORA_RANK], axis=-1)
    q = (rms_norm(cq, q_latent_norm) @ w_uq).reshape(b, s, MLA_HEADS, QK_HEAD_DIM)
    q_nope, q_rope = jnp.split(q, [QK_NOPE_DIM], axis=-1)
    q_rope = apply_rope(q_rope, cos[:, None, :], sin[:, None, :])
    o = mla_attention(q_nope, q_rope, k_nope, k_rope, v).reshape(b, s, MLA_WIDTH)
    return (o * jax.nn.silu(g)) @ w_out

def residual_update(x, out, g_post, p_i, w_pp, w_pg):
    x = x + rms_norm(out, g_post)
    return x + (p_i @ w_pp) * jax.nn.sigmoid(x @ w_pg)

def first_inputs(seed: int = 0) -> dict:
    key = jax.random.key(seed)
    ks = jax.random.split(key, 17)

    def w(k, shape, fan_in):
        return jax.random.normal(k, shape, jnp.float32) * fan_in ** -0.5

    def gain(k, shape):
        return 1.0 + 0.05 * jax.random.normal(k, shape, jnp.float32)

    return {
        "x": jax.random.normal(ks[0], (BATCH, SEQ, D_MODEL), jnp.float32),
        "p": jax.random.normal(ks[1], (DEPTH, BATCH, SEQ, PLE_DIM), jnp.float32),
        "norm_pre": gain(ks[2], (DEPTH, D_MODEL)),
        "norm_post": gain(ks[3], (DEPTH, D_MODEL)),
        "w_in_a": w(ks[4], (N_A, D_MODEL, 4 * SB_WIDTH), D_MODEL),
        "w_out_a": w(ks[5], (N_A, SB_WIDTH, D_MODEL), SB_WIDTH),
        "w_in_b": w(ks[6], (N_B, D_MODEL, Q_LORA_RANK + MLA_WIDTH), D_MODEL),
        "q_latent_norm": gain(ks[7], (N_B, Q_LORA_RANK)),
        "w_uq": w(ks[8], (N_B, Q_LORA_RANK, MLA_HEADS * QK_HEAD_DIM), Q_LORA_RANK),
        "w_out_b": w(ks[9], (N_B, MLA_WIDTH, D_MODEL), MLA_WIDTH),
        "kv_norm": gain(ks[10], (D_MODEL,)),
        "w_dkv": w(ks[11], (D_MODEL, KV_LORA_RANK + QK_ROPE_DIM), D_MODEL),
        "kv_latent_norm": gain(ks[12], (KV_LORA_RANK,)),
        "w_uk": w(ks[13], (KV_LORA_RANK, MLA_HEADS * QK_NOPE_DIM), KV_LORA_RANK),
        "w_uv": w(ks[14], (KV_LORA_RANK, MLA_WIDTH), KV_LORA_RANK),
        "w_ple_proj": w(ks[15], (DEPTH, PLE_DIM, D_MODEL), PLE_DIM),
        "w_ple_gate": w(ks[16], (DEPTH, D_MODEL, D_MODEL), D_MODEL),
    }

def first_block(x, p, norm_pre, norm_post, w_in_a, w_out_a, w_in_b, q_latent_norm, w_uq, w_out_b,
              kv_norm, w_dkv, kv_latent_norm, w_uk, w_uv, w_ple_proj, w_ple_gate):
    cos, sin = rope_tables(x.shape[1])
    for i in range(N_A):
        out = mixer_a(rms_norm(x, norm_pre[i]), w_in_a[i], w_out_a[i])
        x = residual_update(x, out, norm_post[i], p[i], w_ple_proj[i], w_ple_gate[i])
    kv = shared_kv(x, kv_norm, w_dkv, kv_latent_norm, w_uk, w_uv, cos, sin)
    for j in range(N_B):
        i = N_A + j
        out = mixer_b(rms_norm(x, norm_pre[i]), kv, w_in_b[j], q_latent_norm[j], w_uq[j], w_out_b[j], cos, sin)
        x = residual_update(x, out, norm_post[i], p[i], w_ple_proj[i], w_ple_gate[i])
    return x


DEPTH_2 = 1

MIX_WIDTH = D_MODEL
ATTN_WIDTH = MIX_WIDTH // 2
CONV_WIDTH = MIX_WIDTH - ATTN_WIDTH
N_HEADS = 8
HEAD_DIM = ATTN_WIDTH // N_HEADS
QK_DIM = HEAD_DIM // 2
CONV_K = 3
D_FF = ((8 * D_MODEL + 3 * 256 - 1) // (3 * 256)) * 256
N_BUCKETS = 32
MAX_DISTANCE = 128
NORM_EPS = 1e-6
SUBLN_EPS = 1e-5
IN_COLS = 3 * ATTN_WIDTH + 3 * CONV_WIDTH


def rms_norm_2(x, g, eps=NORM_EPS):
    xf = x.astype(jnp.float32)
    y = xf * lax.rsqrt(jnp.mean(xf * xf, axis=-1, keepdims=True) + eps)
    return (y * g.astype(jnp.float32)).astype(x.dtype)

def rel_bucket(dist):
    n = jnp.maximum(dist, 0)
    max_exact = N_BUCKETS // 2
    nf = jnp.maximum(n, max_exact).astype(jnp.float32)
    large = max_exact + (jnp.log(nf / max_exact) / math.log(MAX_DISTANCE / max_exact)
                         * (N_BUCKETS - max_exact)).astype(jnp.int32)
    large = jnp.minimum(large, N_BUCKETS - 1)
    return jnp.where(n < max_exact, n, large)

def diff_attention(q, k, v, lam, rel_bias):
    b, s = q.shape[0], q.shape[1]
    nb = s // Q_BLOCK
    scale = QK_DIM ** -0.5
    k_pos = jnp.arange(s, dtype=jnp.int32)
    q_blocks = q.reshape(b, nb, Q_BLOCK, N_HEADS, 2, QK_DIM).transpose(1, 0, 2, 3, 4, 5)
    starts = jnp.arange(nb, dtype=jnp.int32) * Q_BLOCK

    def block(args):
        q_blk, start = args
        q_pos = start + jnp.arange(Q_BLOCK, dtype=jnp.int32)
        dist = q_pos[:, None] - k_pos[None, :]
        bias = jnp.transpose(rel_bias[rel_bucket(dist)], (2, 0, 1)).astype(jnp.float32)
        logits = jnp.einsum('bqhcd,bkhcd->bhcqk', q_blk, k).astype(jnp.float32) * scale
        logits = logits + bias[None, :, None]
        logits = jnp.where(dist >= 0, logits, -jnp.inf)
        p = jax.nn.softmax(logits, axis=-1)
        w = (p[:, :, 0] - lam * p[:, :, 1]).astype(v.dtype)
        return jnp.einsum('bhqk,bkhe->bqhe', w, v)

    o = lax.map(block, (q_blocks, starts))
    return o.transpose(1, 0, 2, 3, 4).reshape(b, s, N_HEADS, HEAD_DIM)

def short_conv(h, w):
    return lax.conv_general_dilated(
        h, w[:, None, :].astype(h.dtype), window_strides=(1,),
        padding=[(CONV_K - 1, 0)], dimension_numbers=('NWC', 'WIO', 'NWC'),
        feature_group_count=h.shape[-1])

def second_inputs(seed: int = 0) -> dict:
    key = jax.random.key(seed)
    ks = jax.random.split(key, 20)
    f32 = jnp.float32
    nrm = lambda k, shape, s: jax.random.normal(k, shape, f32) * s
    gain = lambda k, shape: 1.0 + 0.05 * jax.random.normal(k, shape, f32)
    return {
        "x": jax.random.normal(ks[0], (BATCH, SEQ, D_MODEL), f32),
        "w_in": nrm(ks[1], (DEPTH_2, D_MODEL, IN_COLS), D_MODEL ** -0.5),
        "w_out": nrm(ks[2], (DEPTH_2, MIX_WIDTH, D_MODEL), MIX_WIDTH ** -0.5),
        "lambda_q1": nrm(ks[3], (DEPTH_2, QK_DIM), 0.1),
        "lambda_k1": nrm(ks[4], (DEPTH_2, QK_DIM), 0.1),
        "lambda_q2": nrm(ks[5], (DEPTH_2, QK_DIM), 0.1),
        "lambda_k2": nrm(ks[6], (DEPTH_2, QK_DIM), 0.1),
        "subln_gain": gain(ks[7], (DEPTH_2, HEAD_DIM)),
        "conv_w": nrm(ks[8], (DEPTH_2, CONV_K, CONV_WIDTH), CONV_K ** -0.5),
        "conv_norm_gain": gain(ks[9], (DEPTH_2, CONV_WIDTH)),
        "rel_bias": nrm(ks[10], (N_BUCKETS, N_HEADS), 0.5),
        "w_gate": nrm(ks[11], (DEPTH_2, D_MODEL, D_FF), D_MODEL ** -0.5),
        "w_up": nrm(ks[12], (DEPTH_2, D_MODEL, D_FF), D_MODEL ** -0.5),
        "w_down": nrm(ks[13], (DEPTH_2, D_FF, D_MODEL), D_FF ** -0.5),
        "norm_mix_pre": gain(ks[14], (DEPTH_2, D_MODEL)),
        "norm_mix_post": gain(ks[15], (DEPTH_2, D_MODEL)),
        "norm_ffn_pre": gain(ks[16], (DEPTH_2, D_MODEL)),
        "norm_ffn_post": gain(ks[17], (DEPTH_2, D_MODEL)),
    }

def second_block(x, w_in, w_out, lambda_q1, lambda_k1, lambda_q2, lambda_k2, subln_gain,
              conv_w, conv_norm_gain, rel_bias, w_gate, w_up, w_down,
              norm_mix_pre, norm_mix_post, norm_ffn_pre, norm_ffn_post):
    b, s, _ = x.shape
    A, C = ATTN_WIDTH, CONV_WIDTH
    split_at = [A, 2 * A, 3 * A, 3 * A + C, 3 * A + 2 * C]
    for l in range(DEPTH_2):
        lambda_init = 0.8 - 0.6 * math.exp(-0.3 * l)
        hn = rms_norm_2(x, norm_mix_pre[l])
        proj = hn @ w_in[l]
        q, k, v, gate_b, gate_c, hc = jnp.split(proj, split_at, axis=-1)
        q = q.reshape(b, s, N_HEADS, 2, QK_DIM)
        k = k.reshape(b, s, N_HEADS, 2, QK_DIM)
        v = v.reshape(b, s, N_HEADS, HEAD_DIM)
        lam = (jnp.exp(jnp.sum(lambda_q1[l].astype(jnp.float32) * lambda_k1[l].astype(jnp.float32)))
               - jnp.exp(jnp.sum(lambda_q2[l].astype(jnp.float32) * lambda_k2[l].astype(jnp.float32)))
               + lambda_init)
        a = diff_attention(q, k, v, lam, rel_bias)
        a = rms_norm_2(a, subln_gain[l], SUBLN_EPS) * (1.0 - lambda_init)
        a = a.reshape(b, s, A)
        c = gate_b * short_conv(gate_c * hc, conv_w[l])
        c = rms_norm_2(c, conv_norm_gain[l])
        mix = jnp.concatenate([a, c], axis=-1) @ w_out[l]
        x = x + rms_norm_2(mix, norm_mix_post[l])
        hn = rms_norm_2(x, norm_ffn_pre[l])
        f = (jax.nn.silu(hn @ w_gate[l]) * (hn @ w_up[l])) @ w_down[l]
        x = x + rms_norm_2(f, norm_ffn_post[l])
    return x


def setup_inputs(seed=0):
    out = dict(first_inputs(seed))
    for name, value in second_inputs(seed + 1).items():
        if name != "x":
            out[name + "_2"] = value
    return out


def reference(
    x, p, norm_pre, norm_post, w_in_a, w_out_a, w_in_b, q_latent_norm, w_uq, w_out_b, kv_norm,
    w_dkv, kv_latent_norm, w_uk, w_uv, w_ple_proj, w_ple_gate, w_in_2, w_out_2, lambda_q1_2,
    lambda_k1_2, lambda_q2_2, lambda_k2_2, subln_gain_2, conv_w_2, conv_norm_gain_2, rel_bias_2,
    w_gate_2, w_up_2, w_down_2, norm_mix_pre_2, norm_mix_post_2, norm_ffn_pre_2,
    norm_ffn_post_2,
):
    x = first_block(
        x, p, norm_pre, norm_post, w_in_a, w_out_a, w_in_b, q_latent_norm, w_uq, w_out_b,
        kv_norm, w_dkv, kv_latent_norm, w_uk, w_uv, w_ple_proj, w_ple_gate,
    )
    return second_block(
        x, w_in_2, w_out_2, lambda_q1_2, lambda_k1_2, lambda_q2_2, lambda_k2_2, subln_gain_2,
        conv_w_2, conv_norm_gain_2, rel_bias_2, w_gate_2, w_up_2, w_down_2, norm_mix_pre_2,
        norm_mix_post_2, norm_ffn_pre_2, norm_ffn_post_2,
    )


_drawn_inputs = setup_inputs


def setup_inputs(seed=0):
    import zlib

    import numpy as np

    out = dict(_drawn_inputs(seed))
    spreads = {}
    factors = {'lambda_q2_2': 8.0,
     'lambda_k2_2': 8.0,
     'subln_gain_2': 31.068,
     'conv_norm_gain_2': 22.538,
     'norm_ffn_post_2': 2.675,
     'lambda_q1_2': 64.0,
     'lambda_k1_2': 8.0}
    for name, (base, spread) in spreads.items():
        noise = np.random.default_rng([zlib.crc32(name.encode()), seed]).standard_normal(out[name].shape)
        drawn = base * np.exp(spread * noise) if base else spread * noise
        out[name] = __import__('jax').numpy.asarray(drawn.astype(out[name].dtype))
    for name, factor in factors.items():
        out[name] = (out[name] * factor).astype(out[name].dtype)
    return out
```

```python
import math
from contextlib import ExitStack

import numpy as np
import concourse.bass as bass
from concourse import mybir

F32 = mybir.dt.float32
F32R = mybir.dt.float32r
BF16 = mybir.dt.bfloat16
ALU = mybir.AluOpType
ACT = mybir.ActivationFunctionType
AX = mybir.AxisListType

P = 128
S = 256
D = 2048
KD = D // P
DFF = 5632
NRAW = 4
NSPL = 4
AHEAD = 3
CH = 1024
CONST = ["ident", "flip", "tri", "ones", "perm", "mask", "cos", "sin", "negA", "negB"]
CW = {"cos": 256, "sin": 256}


class Queue:

    def __init__(self, sem):
        self.sem, self.n, self.ops, self.seen = sem, 0, [], {}

    def wait(self, *tokens):
        for t in tokens:
            if t is None:
                continue
            if isinstance(t, list):
                self.wait(*t)
                continue
            sem, value = t
            if self.seen.get(sem, 0) < value:
                self.seen[sem] = value
                self.ops.append(lambda e, sem=sem, value=value: e.wait_ge(sem, value))

    def do(self, fn, *tokens, inc=True):
        self.wait(*tokens)
        if not inc:
            self.ops.append(fn)
            return None
        self.n += 1
        self.ops.append(lambda e: fn(e).then_inc(self.sem, 1))
        return (self.sem, self.n)

    def dma(self, fn, sem, value, *tokens):
        self.wait(*tokens)
        self.ops.append(lambda e: fn(e).then_inc(sem, 16))
        return (sem, value)

    def play(self, eng):
        for op in self.ops:
            op(eng)


def build(nc, a, cst, onehot, out, stop=None):
    ctx = ExitStack()
    with ctx:
        BASE = 16512
        pos = [BASE]

        def at(name, shape, dt, off):
            return nc.alloc_sbuf_tensor_at(name, shape, dt, offset=off)

        def sb(name, shape, dt=F32):
            n = int(np.prod(shape[1:])) * (2 if dt == BF16 else 4)
            t = at(name, shape, dt, pos[0])
            pos[0] += (n + 31) // 32 * 32
            return t

        xT = sb("xT", [P, KD, S])
        H = sb("H", [P, KD, 2 * S], F32R)
        R1 = pos[0]
        O = at("O", [P, KD, 2 * S], F32R, R1)
        SL = [R1 + 32768 + 18432 * s for s in range(2)]
        qT = [at(f"qT{s}", [P, 4, S], F32, SL[s]) for s in range(2)]
        kT = [at(f"kT{s}", [P, 4, S], F32, SL[s] + 4096) for s in range(2)]
        Vn = [at(f"Vn{s}", [P, 2, 512], F32, SL[s] + 8192) for s in range(2)]
        gT = [at(f"gT{s}", [P, 4, S], F32, SL[s] + 12288) for s in range(2)]
        qR = [at(f"qR{s}", [P, 2, S], F32, SL[s] + 16384) for s in range(2)]
        T = at("T", [P, KD, S], F32, SL[0])
        PP = at("PP", [P, KD, S], F32, SL[1])
        RAWL = at("RAWL", [P, 4, S], F32, SL[1])
        GC = at("GC", [P, 4, S], F32, SL[0])
        CT = at("CT", [P, 8, S], F32, SL[0] + 4096)
        ACTS = at("ACTS", [P, 24, 2 * S], F32R, R1)
        T2 = at("T2", [P, KD, S], F32, R1 + 49152)
        SG = at("SG", [P, 4, S], F32, R1 + 65536)
        XN = at("XN", [P, 2, D], F32, SL[0])
        YN = at("YN", [P, 2, D], F32, R1)
        GN = at("GN", [P, 2, P], F32, SL[1])
        OH = at("OH", [32, 384], F32, SL[1] + 1024)
        RB = at("RB", [32, 8], F32, SL[1] + 2560)
        MR = at("MR", [1, 384], F32, SL[1] + 2592)
        BV = at("BV", [8, 384], F32, SL[1] + 4128)
        LM = at("LM", [1, 4, 64], F32, SL[1] + 5664)
        LP = at("LP", [1, 2, 64], F32, SL[1] + 6688)
        LS = at("LS", [1, 8], F32, SL[1] + 7200)
        NG = at("NG", [P, 2, P], F32, SL[1] + 7232)
        pos[0] = R1 + 69632
        L1 = pos[0]
        CKV = sb("CKV", [P, 4, 2 * S], F32R)
        CQ = sb("CQ", [P, 4, 2 * S], F32R)
        RT = at("RT", [P, 8, S], F32, L1)
        KR = sb("KR", [P, S])
        PN = sb("PN", [P, 2, S])
        RAW = sb("RAW", [P, NRAW, CH])
        WH = sb("WH", [P, NSPL, CH], F32R)
        WL = sb("WL", [P, NSPL, CH], F32R)
        C = {n: sb("c_" + n, [P, CW.get(n, P)]) for n in CONST[:8]}
        identb = sb("identb", [P, P], BF16)
        negb = [sb(f"negb{i}", [P, P], BF16) for i in range(2)]
        GAIN = sb("GAIN", [P, 256])
        NLAM = sb("NLAM", [P, 3])
        TMP = [sb(f"TMP{i}", [P, 2, S]) for i in range(2)]
        TM2 = sb("TM2", [P, 2, S])
        SQ = sb("SQ", [P, 2, S])
        ACC = sb("ACC", [P, 2, S])
        RS = sb("RS", [P, S])
        F1 = sb("F1", [P, 2, 384])
        F2 = sb("F2", [P, 2, 384])
        RV, RW = SQ[:, 0, :], SQ[:, 1, :]
        SM = sb("SM", [P, 16])
        NONES = sb("NONES", [P, P])
        C["negones"] = NONES[:, :]
        if pos[0] > 229344:
            raise ValueError(f"SBUF over by {pos[0] - 229344}")

        ps = ctx.enter_context(nc.psum_tensor("ps", [P, 8, 512], F32))
        bvd = nc.dram_tensor("bvd", (8, 384), F32, kind="Internal").ap()

        def sem(name):
            return ctx.enter_context(nc.semaphore(name))

        s_pe, s_act, s_dve = sem("s_pe"), sem("s_act"), sem("s_dve")
        s_raw = [sem(f"s_raw{i}") for i in range(NRAW)]
        s_in = [sem(f"s_in{i}") for i in range(16)]
        s_out = sem("s_out")

        def program(chunks_known):
            PE, AC, DV, SP = Queue(s_pe), Queue(s_act), Queue(s_dve), Queue(None)
            chunks = []

            def V(fn, *t):
                return DV.do(fn, *t)

            def A(fn, *t):
                return AC.do(fn, *t)

            def act(o, i, f, *t, **kw):
                return A(lambda e: e.activation(o, i, f, **kw), *t)

            def tt(o, x, y, op, *t):
                return V(lambda e: e.tensor_tensor(o, x, y, op), *t)

            def ts(o, x, s1, s2, op0, op1, *t):
                if op1 is None:
                    return V(lambda e: e.tensor_scalar(o, x, s1, None, op0), *t)
                return V(lambda e: e.tensor_scalar(o, x, s1, s2, op0, op1), *t)

            def stt(o, x, s, y, op0, op1, *t):
                return V(lambda e: e.scalar_tensor_tensor(out=o, in0=x, scalar=s, in1=y, op0=op0, op1=op1), *t)

            def mm(o, l, r, start=False, *t, inc=False):
                return PE.do(lambda e: e.matmul(o, l, r, start=start, stop=True, skip_group_check=True), *t, inc=inc)

            def tr(o, i, *t, inc=False):
                idn = C["ident"][:, :] if i.shape[0] == P else C["ident"][0:i.shape[0], 0:i.shape[0]]
                return PE.do(lambda e: e.transpose(o, i, idn), *t, inc=inc)

            small = [0]

            def load(dst, src, q=None, *t):
                i = small[0]
                small[0] += 1
                return (q or AC).dma(lambda e: e.dma_start(dst, src), s_in[i], 16, *t)

            raw_count = [0] * NRAW
            raw_tok, raw_free = {}, {}
            spl_tok, spl_free = {}, {}
            loaded, split = [0], [0]

            def load_chunk():
                i = loaded[0]
                if i >= len(chunks_known):
                    return
                loaded[0] += 1
                slot = i % NRAW
                SP.wait(raw_free.get(i - NRAW))
                for off, n, src in chunks_known[i][0]:
                    dst = RAW[:, slot, off:off + n]
                    raw_count[slot] += 16
                    if len(src.shape) == 3:
                        dst = dst.rearrange("p (a b) -> p a b", a=src.shape[1])
                    raw_tok[i] = SP.dma(lambda e, dst=dst, src=src: e.dma_start(dst, src),
                                        s_raw[slot], raw_count[slot])

            def split_chunk():
                i = split[0]
                if i >= len(chunks_known):
                    return
                split[0] += 1
                r, w, n = i % NRAW, i % NSPL, chunks_known[i][1]
                raw, hi, lo = RAW[:, r, 0:n], WH[:, w, 0:n], WL[:, w, 0:n]
                th = act(hi, raw, ACT.Copy, raw_tok[i], spl_free.get(i - NSPL))
                spl_tok[i] = tt(lo, raw, hi.bitcast(F32), ALU.subtract, th)
                raw_free[i] = [th, spl_tok[i]]
                load_chunk()

            def next_chunk(parts, n):
                i = len(chunks)
                chunks.append((parts, n))
                if chunks_known:
                    while split[0] <= min(i + AHEAD - 1, len(chunks_known) - 1):
                        split_chunk()
                return i

            bg = []

            def bgstep():
                while bg:
                    try:
                        next(bg[0])
                        return
                    except StopIteration:
                        bg.pop(0)

            def drain():
                while bg:
                    bgstep()

            bank_free = {b: None for b in range(8)}
            ring = [0]

            def take(n):
                b = ring[0]
                ring[0] = (b + n) % 6
                return b

            def dense(src, c0, nt, kts, xs, xt, per=2, natural=False, view=None):
                nk = len(kts)
                b0 = take(2 if natural else (nt + 1) // 2 * 2)
                w = nt * P
                toks = []
                for ci in range(0, nk, per):
                    ks = kts[ci:ci + per]
                    if view:
                        parts = [p for j, k in enumerate(ks) for p in view(j, k)]
                    else:
                        parts = [(0, len(ks) * w, src[ks[0] * P:(ks[-1] + 1) * P, c0:c0 + w]
                                  .rearrange("(c p) n -> p c n", p=P))]
                    i = next_chunk(parts, len(ks) * w)
                    if chunks_known:
                        PE.wait(spl_tok[i])
                    hi = WH[:, i % NSPL, 0:len(ks) * w].rearrange("p (c n) -> p c n", n=w)
                    lo = WL[:, i % NSPL, 0:len(ks) * w].rearrange("p (c n) -> p c n", n=w)
                    last_chunk = ci + per >= nk
                    if natural:
                        if ci == 0:
                            PE.wait(bank_free[b0], bank_free[b0 + 1])
                        for j, k in enumerate(ks):
                            n = ci + j
                            PE.wait(xt(n))
                            for t in range(2):
                                xh = xs[:, n, t * P:(t + 1) * P]
                                xl = xs[:, n, S + t * P:S + (t + 1) * P]
                                o = ps[:, b0 + t, :]
                                mm(o, xh, hi[:, j, :], n == 0)
                                mm(o, xh, lo[:, j, :])
                                end = mm(o, xl, hi[:, j, :], inc=(t == 1 and j == len(ks) - 1))
                        if last_chunk:
                            toks.append((b0, end))
                    else:
                        for t in range(nt):
                            b = (b0 + t) % 6
                            if ci == 0:
                                PE.wait(bank_free[b])
                            for j, k in enumerate(ks):
                                n = ci + j
                                PE.wait(xt(n))
                                wh, wl = hi[:, j, t * P:(t + 1) * P], lo[:, j, t * P:(t + 1) * P]
                                mm(ps[:, b, :], wh, xs[:, n, :], n == 0)
                                fin = j == len(ks) - 1 and (t == nt - 1 or (last_chunk and t % 2 == 1))
                                end = mm(ps[:, b, S:2 * S], wl, xs[:, n, 0:S], inc=fin)
                            if last_chunk and (t % 2 == 1 or t == nt - 1):
                                toks.append((b - t % 2, end))
                    spl_free[i] = end
                    bgstep()
                return toks

            def halves(b, n=2):
                return ps[:, b:b + n, 0:S], ps[:, b:b + n, S:2 * S]

            def release(b, tok, n=2):
                for i in range(n):
                    bank_free[b + i] = tok

            def sum_pair(o, b, tok, *t, n=2):
                x, y = halves(b, n)
                r = act(o, y, ACT.Copy, tok, *t)
                r = tt(o, x, o, ALU.add, r)
                release(b, r, n)
                return r

            tmp_free = [None, None]
            tmp_at = [0]

            def tmp():
                i = tmp_at[0]
                tmp_at[0] = 1 - i
                return i, TMP[i]

            def bc(ap, n=2):
                return ap.unsqueeze(1).broadcast_to([P, n, ap.shape[-1]])

            def split_x(src, dst, k0, n, dep, *war):
                th = act(dst[:, k0:k0 + n, 0:S], src, ACT.Copy, dep, *war)
                return tt(dst[:, k0:k0 + n, S:2 * S], src, dst[:, k0:k0 + n, 0:S].bitcast(F32),
                          ALU.subtract, th)

            st = {"first": True, "acc": None, "accfree": None, "sq": None, "rs": None}

            def sq_add(src, dep):
                if st["first"]:
                    st["acc"] = act(ACC[:, :, :], src, ACT.Square, dep, st["accfree"])
                    st["first"] = False
                    return st["acc"]
                t = act(SQ[:, :, :], src, ACT.Square, dep, st["sq"])
                st["acc"] = st["sq"] = tt(ACC[:, :, :], ACC[:, :, :], SQ[:, :, :], ALU.add, t, st["acc"])
                return t

            def rstd(dim, eps, *war):
                drain()
                PE.wait(bank_free[6], st["acc"])
                mm(ps[:, 6, 0:S], C["ones"][:, :], ACC[:, 0, :], True)
                t = mm(ps[:, 6, 0:S], C["ones"][:, :], ACC[:, 1, :], inc=True)
                st["accfree"], st["first"] = t, True
                t = ts(RV, ps[:, 6, 0:S], 1.0 / dim, eps, ALU.mult, ALU.add, t, *war)
                bank_free[6] = t
                st["sq"] = rsqrt(RS[:, :], RV, RW, t)
                return st["sq"]

            def rsqrt(o, v, w, dep):
                t = act(w, v, ACT.Ln, dep)
                t = act(o, w, ACT.Exp, t, scale=-0.5)
                t = stt(w, o, -0.5, o, ALU.mult, ALU.mult, t)
                t = tt(w, w, v, ALU.mult, t)
                return stt(o, w, 1.5, o, ALU.add, ALU.mult, t)

            def norm_to(src, g0, dst, n, r, *war):
                toks = []
                for c in range(0, n, 2):
                    i, tm = tmp()
                    for j in range(2):
                        t = stt(tm[:, j, :], src[:, c + j, :], GAIN[:, g0 + c + j:g0 + c + j + 1], RS[:, :],
                                ALU.mult, ALU.mult, r, tmp_free[i])
                    t = split_x(tm[:, :, :], dst, c, 2, t, *war)
                    tmp_free[i] = t
                    toks += [t, t]
                return toks

            def silu(o, x, dep, scratch, *war):
                t = act(scratch, x, ACT.Exp, dep, *war, scale=-1.0)
                t = ts(scratch, scratch, 1.0, None, ALU.add, None, t)
                t = V(lambda e: e.reciprocal(scratch, scratch), t)
                return tt(o, x, scratch, ALU.mult, t, dep)

            off = 0
            cl = []
            for n in CONST:
                w = CW.get(n, P)
                if n in CONST[:8]:
                    cl.append((C[n][:, :], off, w))
                else:
                    cl.append((NG[:, CONST.index(n) - 8, :], off, w))
                off += w
            t_ident = load(cl[0][0], cst[:, 0:P], SP)
            t_x = load(XN[:, :, :], a["x"].rearrange("a (t p) d -> p (a t) d", p=P), SP)
            i = small[0]
            small[0] += 1
            for n_, (dst, o_, w) in enumerate(cl[1:]):
                t_cst = AC.dma(lambda e, dst=dst, o_=o_, w=w: e.dma_start(dst, cst[:, o_:o_ + w]), s_in[i],
                               16 * (n_ + 1))
            i = small[0]
            small[0] += 1
            gi = [0]
            gcol = {}

            def grow(name, src, rows):
                if gi[0] < P < gi[0] + rows:
                    gi[0] = P
                r = gi[0]
                gcol[name] = r
                gi[0] += rows
                load_rows.append((GN[r % P:r % P + rows, r // P, 0:src.shape[-1]], src))

            load_rows = []
            r16 = lambda v: v.rearrange("(c p) -> c p", p=P)
            for l in range(2):
                grow(f"pre{l}", r16(a["norm_pre"][l]), 16)
            grow("mixpre", r16(a["norm_mix_pre_2"][0]), 16)
            for l in range(2):
                grow(f"post{l}", r16(a["norm_post"][l]), 16)
            grow("kv", r16(a["kv_norm"]), 16)
            grow("mixpost", r16(a["norm_mix_post_2"][0]), 16)
            grow("ffnpre", r16(a["norm_ffn_pre_2"][0]), 16)
            grow("ffnpost", r16(a["norm_ffn_post_2"][0]), 16)
            grow("ckv", r16(a["kv_latent_norm"]), 4)
            grow("cq", r16(a["q_latent_norm"][0]), 4)
            for j in range(3):
                grow(f"cw{j}", r16(a["conv_w_2"][0, j]), 8)
            grow("cn", r16(a["conv_norm_gain_2"][0]), 8)
            grow("sub", a["subln_gain_2"], 1)
            for n_, (dst, src) in enumerate(load_rows):
                t_g = AC.dma(lambda e, dst=dst, src=src: e.dma_start(dst, src), s_in[i], 16 * (n_ + 1))
            nrow2 = gi[0] - P
            t_p = load(PN[:, :, :], a["p"][0, 0].rearrange("(t p) d -> p t d", p=P))
            t_oh = load(OH[:, :], onehot[0:32, :])
            t_mr = load(MR[:, :], onehot[32:33, :])
            t_rb = load(RB[:, :], a["rel_bias_2"])
            i = small[0]
            small[0] += 1
            for n_, nm in enumerate(["q1", "k1", "q2", "k2"]):
                t_lm = AC.dma(lambda e, n_=n_, nm=nm: e.dma_start(LM[:, n_, :], a[f"lambda_{nm}_2"]), s_in[i],
                              16 * (n_ + 1))
            if chunks_known:
                for _ in range(NRAW):
                    load_chunk()

            t_xt = []
            for c in range(0, KD, 2):
                b = take(2)
                for j in range(2):
                    PE.wait(bank_free[b + j])
                    for t in range(2):
                        e_ = tr(ps[:, b + j, t * P:(t + 1) * P], XN[:, t, (c + j) * P:(c + j + 1) * P],
                                t_ident, t_x, inc=(j == 1 and t == 1))
                t_v = V(lambda e, b=b, c=c: e.tensor_copy(xT[:, c:c + 2, :], ps[:, b:b + 2, 0:S]), e_)
                release(b, t_v)
                t_xt.append(t_v)
                sq_add(xT[:, c:c + 2, :], t_v)
            PE.wait(bank_free[7], t_g)
            tr(ps[:, 7, 0:P], GN[:, 0, :])
            t = tr(ps[:, 7, P:P + nrow2], GN[0:nrow2, 1, :], inc=True)
            t_gain = V(lambda e: e.tensor_copy(GAIN[:, 0:P + nrow2], ps[:, 7, 0:P + nrow2]), t)
            s0 = gcol["sub"]
            t_gain = ts(GAIN[:, s0:s0 + 1], GAIN[:, s0:s0 + 1], 0.8, None, ALU.mult, None, t_gain)
            bank_free[7] = t_gain
            r = rstd(D, 1e-6, t_cst)

            def p_split(t_p):
                drain()
                PE.wait(bank_free[7], t_p)
                for k in range(2):
                    for t in range(2):
                        e_ = tr(ps[:, 7, k * S + t * P:k * S + (t + 1) * P], PN[:, t, k * P:(k + 1) * P],
                                inc=(k == 1 and t == 1))
                i, tm = tmp()
                t = V(lambda e: e.tensor_copy(tm[:, :, :], ps[:, 7, :].rearrange("p (k s) -> p k s", k=2)),
                      e_, tmp_free[i])
                bank_free[7] = t
                t = split_x(tm[:, :, :], CQ, 0, 2, t)
                tmp_free[i] = t
                return [e_, t]

            t_h = norm_to(xT, gcol["pre0"], H, KD, [r, t_gain])

            def setup_late():
                V(lambda e: e.tensor_copy(identb[:, :], C["ident"][:, :]), t_cst)
                for j in range(2):
                    V(lambda e, j=j: e.tensor_copy(negb[j][:, :], NG[:, j, :]))
                PE.wait(bank_free[6], t_oh, t_rb, t_mr)
                mm(ps[0:8, 6, 0:384], RB[:, :], OH[:, :], True)
                t = mm(ps[0:8, 6, 0:384], C["ones"][0:1, 0:8], MR[:, :], inc=True)
                t = V(lambda e: e.tensor_copy(BV[:, :], ps[0:8, 6, 0:384]), t)
                bank_free[6] = t
                t_bv = load(bvd, BV[:, :], SP, t)
                t = tt(LP[:, :, :], LM[:, 0:4:2, :], LM[:, 1:4:2, :], ALU.mult, t_lm)
                t = V(lambda e: e.tensor_reduce(LS[:, 0:2], LP[:, :, :], AX.X, ALU.add), t)
                t = act(LS[:, 2:4], LS[:, 0:2], ACT.Exp, t)
                t = tt(LS[:, 4:5], LS[:, 3:4], LS[:, 2:3], ALU.subtract, t)
                t = ts(LS[:, 4:5], LS[:, 4:5], -(0.8 - 0.6 * math.exp(0.0)), None, ALU.add, None, t)
                t = stt(LS[:, 7:8], LS[:, 4:5], -1.0, LS[:, 4:5], ALU.mult, ALU.max, t)
                t = ts(LS[:, 7:8], LS[:, 7:8], 1.0, None, ALU.max, None, t)
                t = V(lambda e: e.reciprocal(LS[:, 5:6], LS[:, 7:8]), t)
                t = tt(LS[:, 4:5], LS[:, 4:5], LS[:, 5:6], ALU.mult, t)
                t = stt(LS[:, 6:7], LS[:, 5:6], 1e-5, LS[:, 5:6], ALU.mult, ALU.mult, t)
                PE.wait(bank_free[7], t)
                t = mm(ps[:, 7, 0:3], C["ones"][0:1, :], LS[:, 4:7], True, inc=True)
                t = V(lambda e: e.tensor_copy(NLAM[:, :], ps[:, 7, 0:3]), t)
                bank_free[7] = t
                return t_bv

            t_bv = setup_late()
            ps_tok = p_split(t_p)
            pn_free, p_tok = ps_tok
            o_tok = {}
            slot_pe = [None, None]

            f_free = {"F1": None, "F2": None}

            def pv(slot, vi, nb, w_tok, fin):
                for j in range(nb):
                    PE.wait(w_tok)
                    vc = (vi + j) * P
                    mm(ps[:, 6 + j, 0:S], Vn[slot][:, 0, vc:vc + P], F1[:, j, 0:S], True)
                    t = mm(ps[:, 6 + j, P:S], Vn[slot][:, 1, vc:vc + P], F1[:, j, S:384], inc=(j == nb - 1))
                f_free["F1"] = t
                slot_pe[slot] = t
                return t

            def gate_out(slot, gi_, h0, t, g_tok):
                i, tm = tmp()
                t = tt(tm[:, :, :], ps[:, 6:8, 0:S], gT[slot][:, gi_:gi_ + 2, :], ALU.mult, t, g_tok, tmp_free[i])
                release(6, t)
                t = split_x(tm[:, :, :], O, h0, 2, t)
                tmp_free[i] = t
                o_tok[h0] = o_tok[h0 + 1] = t

            def attn_a(slot, h0, i0, toks):
                PE.wait(bank_free[6], bank_free[7], toks)
                for j in range(2):
                    q, k = qT[slot][:, i0 + j, :], kT[slot][:, i0 + j, :]
                    mm(ps[:, 6 + j, 0:S], k[:, 0:P], q, True)
                    t = mm(ps[:, 6 + j, S:384], k[:, P:S], q[:, P:S], inc=(j == 1))
                yield
                z = ps[:, 6:8, 0:384]
                t = act(F1[:, :, :], z, ACT.Abs, t, f_free["F1"])
                t = act(F1[:, :, :], F1[:, :, :], ACT.Exp, t, scale=-1.0)
                t = act(F1[:, :, :], F1[:, :, :], ACT.Ln, t, bias=1.0)
                yield
                t = stt(F2[:, :, :], z, 0.0, F1[:, :, :], ALU.max, ALU.add, t, f_free["F2"])
                for c in (0, S):
                    d = F2[:, :, c:c + P]
                    t = tt(d, d, bc(C["mask"][:, :]), ALU.mult, t)
                yield
                yield
                PE.wait(t)
                for j in range(2):
                    b = 6 + j
                    mm(ps[:, b, 0:384], C["tri"][:, :], F2[:, j, :])
                    mm(ps[:, b, P:S], C["negones"], F2[:, j, S:384])
                    for c in (0, S):
                        t = mm(ps[:, b, c:c + P], identb[:, :], negb[0][:, :], inc=(j == 1 and c == S))
                f_free["F2"] = t
                yield
                t = act(F1[:, :, :], z, ACT.Exp, t)
                yield
                yield
                t = pv(slot, i0, 2, t, None)
                yield
                gate_out(slot, i0, h0, t, toks)

            def softmax(b0, n, scale, t, lam=None):
                V(lambda e: e.tensor_reduce(SM[:, 0:n], ps[:, b0:b0 + n, 0:P], AX.X, ALU.max), t, f_free["SM"])
                t = V(lambda e: e.tensor_reduce(SM[:, 2:2 + n], ps[:, b0:b0 + n, P:384], AX.X, ALU.max))
                t = ts(SM[:, 4:8], SM[:, 0:4], -scale, None, ALU.mult, None, t)
                for j in range(n):
                    for q in range(2):
                        c0, c1 = (0, P) if q == 0 else (P, 384)
                        cc = 2 * q + j
                        tn = A(lambda e, j=j, c0=c0, c1=c1, cc=cc: e.activation(
                            F2[:, j, c0:c1], ps[:, b0 + j, c0:c1], ACT.Exp, bias=SM[:, 4 + cc:5 + cc],
                            scale=scale, accum_out=SM[:, 8 + cc:9 + cc]), t, f_free["F2"])
                t = V(lambda e: e.reciprocal(SM[:, 12:16], SM[:, 8:12]), tn)
                return t

            f_free["SM"] = None

            def turn(j, t):
                PE.wait(t)
                tr(ps[:, 6 + j, 0:P], F2[:, j, 0:P])
                tr(ps[:, 6 + j, P:S], F2[:, j, P:S])
                return tr(ps[:, 6 + j, S:384], F2[:, j, S:384], inc=True)

            def attn_b(slot, h0, i0, toks, kr_tok):
                PE.wait(bank_free[6], bank_free[7], toks, kr_tok)
                for j in range(2):
                    b, i = 6 + j, i0 + j
                    q, k = qT[slot][:, i, :], kT[slot][:, i, :]
                    r0 = 64 * (i % 2)
                    qr, kr = qR[slot][r0:r0 + 64, i // 2, :], KR[r0:r0 + 64, :]
                    mm(ps[:, b, 0:P], q[:, 0:P], k[:, 0:P], True)
                    mm(ps[:, b, P:384], q[:, P:S], k)
                    mm(ps[:, b, 0:P], qr[:, 0:P], kr[:, 0:P])
                    mm(ps[:, b, P:384], qr[:, P:S], kr)
                    mm(ps[:, b, 0:P], identb[:, :], negb[1][:, :])
                    t = mm(ps[:, b, S:384], identb[:, :], negb[1][:, :], inc=(j == 1))
                yield
                t = softmax(6, 2, 192 ** -0.5, t)
                for j in range(2):
                    for q in range(2):
                        c0, c1 = (0, P) if q == 0 else (P, 384)
                        cc = 12 + 2 * q + j
                        t = ts(F2[:, j, c0:c1], F2[:, j, c0:c1], SM[:, cc:cc + 1], None, ALU.mult, None, t)
                yield
                yield
                turn(0, t)
                t = turn(1, t)
                f_free["F2"] = t
                yield
                t = act(F1[:, :, :], ps[:, 6:8, 0:384], ACT.Copy, t, f_free["F1"])
                yield
                t = pv(slot, i0, 2, t, None)
                yield
                gate_out(slot, i0, h0, t, toks)

            def attn_c(slot, h, i, toks, rt_tok):
                PE.wait(bank_free[6], bank_free[7], toks, rt_tok)
                for j in range(2):
                    b, r0 = 6 + j, 64 * j
                    q, k = qT[slot][r0:r0 + 64, i, :], kT[slot][r0:r0 + 64, i, :]
                    mm(ps[:, b, 0:P], q[:, 0:P], k[:, 0:P], True)
                    mm(ps[:, b, P:384], q[:, P:S], k)
                    mm(ps[:, b, 0:P], C["flip"][:, :], RT[:, h, P:S])
                    t = mm(ps[:, b, P:384], C["flip"][:, :], RT[:, h, :], inc=(j == 1))
                yield
                t = softmax(6, 2, 1.0, t)
                t2 = ts(SM[:, 0:2], SM[:, 13:16:2], NLAM[:, 0:1], None, ALU.mult, None, t)
                t2 = ts(SM[:, 2:4], SM[:, 12:16:2], NLAM[:, 1:2], None, ALU.mult, None, t2)
                for q in range(2):
                    c0, c1 = (0, P) if q == 0 else (P, 384)
                    t = ts(F2[:, 0, c0:c1], F2[:, 0, c0:c1], SM[:, 2 + q:3 + q], None, ALU.mult,
                           None, t2)
                for q in range(2):
                    c0, c1 = (0, P) if q == 0 else (P, 384)
                    t = stt(F2[:, 0, c0:c1], F2[:, 1, c0:c1], SM[:, q:q + 1], F2[:, 0, c0:c1],
                            ALU.mult, ALU.add, t)
                yield
                t = turn(0, t)
                f_free["F2"] = t
                yield
                t = act(F1[:, 0, :], ps[:, 6, 0:384], ACT.Copy, t, f_free["F1"])
                yield
                t = pv(slot, i, 1, t, None)
                yield
                i_, tm = tmp()
                t = V(lambda e: e.tensor_copy(tm[:, 0, :], ps[:, 6, 0:S]), t, tmp_free[i_])
                release(6, t, 1)
                t = tt(tm[:, 1, :], tm[:, 0, :], tm[:, 0, :], ALU.mult, t)
                yield
                t = mm(ps[:, 7, 0:S], C["ones"][:, :], tm[:, 1, :], True, t, inc=True)
                t = ts(F1[:, 0, 0:S], ps[:, 7, 0:S], 1.0 / P, NLAM[:, 2:3], ALU.mult, ALU.add, t)
                release(7, t, 1)
                t = ts(F1[:, 0, 0:S], F1[:, 0, 0:S], 2.0 ** -63, None, ALU.max, None, t)
                t = rsqrt(tm[:, 1, :], F1[:, 0, 0:S], F1[:, 1, 0:S], t)
                s_ = gcol["sub"]
                t = stt(tm[:, 0, :], tm[:, 0, :], GAIN[:, s_:s_ + 1], tm[:, 1, :], ALU.mult, ALU.mult, t)
                th = act(O[:, h, 0:S], tm[:, 0, :], ACT.Copy, t)
                t = tt(O[:, h, S:2 * S], tm[:, 0, :], O[:, h, 0:S].bitcast(F32), ALU.subtract, th)
                tmp_free[i_] = t
                o_tok[h] = t

            def o_ready(n):
                while n not in o_tok:
                    bgstep()
                return o_tok[n]

            def proj(src, c0, xs, xt, dst, nk=KD, scale=None, natural=False, free=None, wk=None, view=None, nt=4):
                toks = dense(src, c0, nt, list(range(nk)), xs, xt, natural=natural, view=view, per=2 if wk is None else wk)
                if natural:
                    b, t = toks[0]
                    t = act(dst, ps[:, b:b + 2, :], ACT.Copy, t, free)
                    release(b, t)
                    return t
                outs = []
                for n_, (b, t) in enumerate(toks):
                    d = dst[:, 2 * n_:2 * n_ + 2, :]
                    if scale is None:
                        outs.append(sum_pair(d, b, t, free))
                    else:
                        i, tm = tmp()
                        t = sum_pair(tm[:, :, :], b, t, tmp_free[i])
                        t = act(d, tm[:, :, :], ACT.Copy, t, free, scale=scale)
                        tmp_free[i] = t
                        outs.append(t)
                return outs

            tm2_free = [None]

            def gate_proj(src, c0, xs, xt, slot, free):
                toks = dense(src, c0, 4, list(range(KD)), xs, xt)
                outs = []
                for n_, (b, t) in enumerate(toks):
                    i, tm = tmp()
                    t = sum_pair(tm[:, :, :], b, t, tmp_free[i])
                    t = silu(gT[slot][:, 2 * n_:2 * n_ + 2, :], tm[:, :, :], t, TM2[:, :, :], free, tm2_free[0])
                    tm2_free[0] = t
                    tmp_free[i] = t
                    outs.append(t)
                return outs

            def out_proj(src, kts, xs, xt, dst, first=True, last=True, per=2, each=None):
                for m in range(4):
                    toks = dense(src, 512 * m, 4, kts, xs, xt, per=per)
                    for n_, (b, t) in enumerate(toks):
                        c = 4 * m + 2 * n_
                        d = dst[:, c:c + 2, :]
                        if first:
                            t = sum_pair(d, b, t)
                        else:
                            i, tm = tmp()
                            t = sum_pair(tm[:, :, :], b, t, tmp_free[i])
                            tmp_free[i] = t = tt(d, d, tm[:, :, :], ALU.add, t)
                        if last:
                            sq_add(d, t)
                    if each:
                        each(m)

            def residual(src, g0, r, sq, split_to=None, war=None, x_toks=None):
                outs = []
                for c in range(0, KD, 2):
                    i, tm = tmp()
                    for j in range(2):
                        t = stt(tm[:, j, :], src[:, c + j, :], GAIN[:, g0 + c + j:g0 + c + j + 1], RS[:, :],
                                ALU.mult, ALU.mult, r, tmp_free[i])
                    t = tt(xT[:, c:c + 2, :], xT[:, c:c + 2, :], tm[:, :, :], ALU.add, t, st.get("xr"))
                    tmp_free[i] = t
                    if sq:
                        sq_add(xT[:, c:c + 2, :], t)
                    if split_to is not None:
                        t = split_x(xT[:, c:c + 2, :], split_to, c, 2, t, war)
                    outs += [t, t]
                    yield outs

            def mixer_tail(l, w_out, wpp, wpg):
                out_proj(w_out, list(range(KD)), O, o_ready, T)
                pp_tok = []
                h_dead = (s_pe, PE.n)

                def pp(m):
                    toks = dense(wpp, 512 * m, 4, [0, 1], CQ, lambda n: p_tok_now[0])
                    for n_, (b, t) in enumerate(toks):
                        pp_tok.append(sum_pair(PP[:, 4 * m + 2 * n_:4 * m + 2 * n_ + 2, :], b, t, slot_pe[1]))

                pp(0)
                r = rstd(D, 1e-6)
                x_tok = []
                steps = residual(T, gcol[f"post{l}"], r, False, H, h_dead)
                for m in range(1, 4):
                    x_tok = next(steps)
                    x_tok = next(steps)
                    pp(m)
                for x_tok in steps:
                    pass
                t_last = None
                for m in range(4):
                    toks = dense(wpg, 512 * m, 4, list(range(KD)), H, lambda n: x_tok[n])
                    for n_, (b, t) in enumerate(toks):
                        c = 4 * m + 2 * n_
                        i, tm = tmp()
                        t = sum_pair(tm[:, :, :], b, t, tmp_free[i])
                        t = act(tm[:, :, :], tm[:, :, :], ACT.Exp, t, scale=-1.0)
                        t = ts(tm[:, :, :], tm[:, :, :], 1.0, None, ALU.add, None, t)
                        t = V(lambda e, tm=tm: e.reciprocal(tm[:, :, :], tm[:, :, :]), t)
                        t = tt(tm[:, :, :], tm[:, :, :], PP[:, c:c + 2, :], ALU.mult, t, pp_tok[c // 2])
                        t = tt(xT[:, c:c + 2, :], xT[:, c:c + 2, :], tm[:, :, :], ALU.add, t)
                        tmp_free[i] = t
                        st["xr"] = sq_add(xT[:, c:c + 2, :], t)
                return (s_pe, PE.n)

            w = a["w_in_a"][0]
            th_ = lambda n: t_h[n]
            qs = 128 ** -0.5
            late = [None, None]
            for j in range(4):
                s = j % 2
                if j >= 2:
                    while 4 * (j - 2) + 3 not in o_tok:
                        bgstep()
                fr = [slot_pe[s], late[s]]
                tq = proj(w, 512 * j, H, th_, qT[s], scale=qs, free=fr)
                tk = proj(w, D + 512 * j, H, th_, kT[s], free=fr)
                tv = proj(w, 2 * D + 512 * j, H, th_, Vn[s][:, :, :], natural=True, free=fr)
                tg = gate_proj(w, 3 * D + 512 * j, H, th_, s, fr)
                for i0 in (0, 2):
                    bg.append(attn_a(s, 4 * j + i0, i0, [tq, tk, tv, tg]))
            p_tok_now = [p_tok]
            if stop == "o_a":
                drain()
            dead = mixer_tail(0, a["w_out_a"][0], a["w_ple_proj"][0], a["w_ple_gate"][0])
            if stop != "a":
                t_p1 = load(PN[:, :, :], a["p"][1, 0].rearrange("(t p) d -> p t d", p=P), SP, pn_free)
                r = rstd(D, 1e-6)
                t_o = norm_to(xT, gcol["kv"], O, KD, r)
                wd = a["w_dkv"]
                def latent(src, c0, xs, xt, gname, dst, between):
                    toks = dense(src, c0, 4, list(range(KD)), xs, xt)
                    for n_, (b, t) in enumerate(toks):
                        t = sum_pair(RAWL[:, 2 * n_:2 * n_ + 2, :], b, t)
                        sq_add(RAWL[:, 2 * n_:2 * n_ + 2, :], t)
                    between()
                    r = rstd(512, 1e-6)
                    return norm_to(RAWL, gcol[gname], dst, 4, r, p_tok)
                hb = {}
                kr_t = {}

                def krope():
                    def view(j, k):
                        src = wd[k * P:(k + 1) * P, 512:576]
                        return [(j * P, 64, src), (j * P + 64, 64, src)]
                    [(b, t)] = dense(None, 0, 1, list(range(KD)), O, lambda n: t_o[n], per=8, view=view)
                    t = sum_pair(KR[:, :].unsqueeze(1), b, t, n=1)
                    kr_t["raw"] = t

                def rope(x, dst, t, *war):
                    PE.wait(bank_free[7], t)
                    e_ = mm(ps[:, 7, 0:S], C["perm"][:, :], x, True, inc=True)
                    i, tm = tmp()
                    t = tt(tm[:, 1, :], ps[:, 7, 0:S], C["sin"][:, :], ALU.mult, e_, tmp_free[i])
                    bank_free[7] = t
                    tc_ = tt(tm[:, 0, :], x, C["cos"][:, :], ALU.mult)
                    t = tt(dst, tm[:, 0, :], tm[:, 1, :], ALU.add, t, tc_, *war)
                    tmp_free[i] = t
                    return t

                t_hb = []
                steps_h = []

                def after_ckv():
                    krope()
                    t_hb.extend(norm_to(xT, gcol["pre1"], H, KD, r, dead))
                    st["hb"] = t_hb[-1]
                t_ckv = latent(wd, 0, O, lambda n: t_o[n], "ckv", CKV, after_ckv)
                kr_tok = rope(KR[:, :], KR[:, :], kr_t["raw"])
                t_cq = latent(a["w_in_b"][0], 0, H, lambda n: t_hb[n], "cq", CQ, lambda: None)
                t_lat = t_cq[-1]
                w_uq = a["w_uq"][0].rearrange("r (h e) -> r h e", e=192)
                slot_pe = slot_pe
                o_tok.clear()
                for j in range(4):
                    s = j % 2
                    if j >= 2:
                        while 4 * (j - 2) + 3 not in o_tok:
                            bgstep()
                    fr = [slot_pe[s], t_lat]
                    tk = proj(a["w_uk"], 512 * j, CKV, lambda n: t_ckv[n], kT[s], nk=4, free=fr)
                    tv = proj(a["w_uv"], 512 * j, CKV, lambda n: t_ckv[n], Vn[s][:, :, :], nk=4, natural=True, free=fr)
                    vq = lambda jj, k, j=j: [(jj * 512, 512, w_uq[k * P:(k + 1) * P, 4 * j:4 * j + 4, 0:128])]
                    tq = proj(None, 0, CQ, lambda n: t_cq[n], qT[s], nk=4, free=fr, view=vq)
                    vr = lambda jj, k, j=j: [(jj * 256, 256, w_uq[k * P:(k + 1) * P, 4 * j:4 * j + 4, 128:192])]
                    tr_ = proj(None, 0, CQ, lambda n: t_cq[n], qR[s], nk=4, free=fr, view=vr, wk=4, nt=2)
                    tg = gate_proj(a["w_in_b"][0], 512 + 512 * j, H, lambda n: t_hb[n], s, fr)

                    def rope_q(s=s, tr_=tr_):
                        for i in range(2):
                            t = rope(qR[s][:, i, :], qR[s][:, i, :], tr_)
                            qr_tok[s] = t
                            yield
                    qr_tok = {}
                    bg.append(rope_q())
                    for i0 in (0, 2):
                        def both(i0=i0, s=s, j=j, toks=[tk, tv, tq, tr_, tg], qq=qr_tok):
                            yield from attn_b(s, 4 * j + i0, i0, toks + [qq[s]], kr_tok)
                        bg.append(both())
                pn2, p_tok2 = None, None
                w_in_done = (s_pe, PE.n)

                def late_p():
                    pass
                if True:
                    drain()
                    PE.wait(bank_free[7], t_p1)
                    for k in range(2):
                        for t_ in range(2):
                            e_ = tr(ps[:, 7, k * S + t_ * P:k * S + (t_ + 1) * P], PN[:, t_, k * P:(k + 1) * P],
                                    inc=(k == 1 and t_ == 1))
                    i, tm = tmp()
                    t = V(lambda e: e.tensor_copy(tm[:, :, :], ps[:, 7, :].rearrange("p (k s) -> p k s", k=2)),
                          e_, tmp_free[i])
                    bank_free[7] = t
                    t = split_x(tm[:, :, :], CQ, 0, 2, t, w_in_done)
                    tmp_free[i] = t
                    p_tok_now[0] = t
                dead = mixer_tail(1, a["w_out_b"][0], a["w_ple_proj"][1], a["w_ple_gate"][1])
            if stop not in ("a", "b"):
                i = small[0]
                small[0] += 1
                SP.wait(t_bv, p_tok_now[0], dead)
                for h in range(8):
                    src = bass.AP(bvd.tensor, h * 384, [[1, P], [1, S]])
                    rt_tok = SP.dma(lambda e, h=h, src=src: e.dma_start(RT[:, h, :], src), s_in[i], 16 * (h + 1))
                r = rstd(D, 1e-6)
                t_h2 = norm_to(xT, gcol["mixpre"], H, KD, r, dead)
                th2 = lambda n: t_h2[n]
                w = a["w_in_2"][0]
                o_tok.clear()
                xfree = (s_dve, DV.n)
                o_dead = dead
                for j in range(2):
                    fr = [slot_pe[j], xfree]
                    tq = proj(w, 512 * j, H, th2, qT[j], scale=0.125, free=fr)
                    tk = proj(w, 1024 + 512 * j, H, th2, kT[j], free=fr)
                    tv = proj(w, 2048 + 512 * j, H, th2, Vn[j][:, :, :], natural=True, free=fr)
                    for i in range(4):
                        bg.append(attn_c(j, 4 * j + i, i, [tq, tk, tv], rt_tok))
                ct_tok = []
                for m in range(2):
                    while m == 0 and 3 not in o_tok:
                        bgstep()
                    tg_ = proj(w, 4096 + 512 * m, H, th2, GC, free=[slot_pe[0]])
                    toks = dense(w, 5120 + 512 * m, 4, list(range(KD)), H, th2)
                    for n_, (b, t) in enumerate(toks):
                        i, tm = tmp()
                        t = sum_pair(tm[:, :, :], b, t, tmp_free[i])
                        g = GC[:, 2 * n_:2 * n_ + 2, :]
                        tmp_free[i] = t_u = tt(g, g, tm[:, :, :], ALU.mult, t, tg_)
                    toks = dense(w, 3072 + 512 * m, 4, list(range(KD)), H, th2)
                    for n_, (b, t) in enumerate(toks):
                        i, tm = tmp()
                        tb_ = sum_pair(tm[:, :, :], b, t, tmp_free[i])
                        for jj in range(2):
                            ch = 4 * m + 2 * n_ + jj
                            u, y = GC[:, 2 * n_ + jj, :], CT[:, ch, :]
                            cw = [GAIN[:, gcol[f"cw{q}"] + ch:gcol[f"cw{q}"] + ch + 1] for q in range(3)]
                            t = ts(y, u, cw[2], None, ALU.mult, None, t_u)
                            t = stt(y[:, 1:S], u[:, 0:S - 1], cw[1], y[:, 1:S], ALU.mult, ALU.add, t)
                            t = stt(y[:, 2:S], u[:, 0:S - 2], cw[0], y[:, 2:S], ALU.mult, ALU.add, t)
                        c2 = CT[:, 4 * m + 2 * n_:4 * m + 2 * n_ + 2, :]
                        t = tt(c2, c2, tm[:, :, :], ALU.mult, t, tb_)
                        tmp_free[i] = t
                        sq_add(c2, t)
                r = rstd(1024, 1e-6)
                cn = gcol["cn"]
                for c in range(0, 8, 2):
                    i, tm = tmp()
                    for j in range(2):
                        t = stt(tm[:, j, :], CT[:, c + j, :], GAIN[:, cn + c + j:cn + c + j + 1], RS[:, :],
                                ALU.mult, ALU.mult, r, tmp_free[i])
                    t = split_x(tm[:, :, :], O, 8 + c, 2, t)
                    tmp_free[i] = t
                    o_tok[8 + c] = o_tok[9 + c] = t
                h_dead = (s_pe, PE.n)
                out_proj(a["w_out_2"][0], list(range(KD)), O, o_ready, T)
                r = rstd(D, 1e-6)
                for x_tok in residual(T, gcol["mixpost"], r, True):
                    pass
            if stop not in ("a", "b", "c"):
                r2 = rstd(D, 1e-6)
                t_h3 = norm_to(xT, gcol["ffnpre"], H, KD, r2, h_dead)
                th3 = lambda n: t_h3[n]
                wg, wu, wdn = a["w_gate_2"][0], a["w_up_2"][0], a["w_down_2"][0]
                acts_free = (s_pe, PE.n)
                for part, (f0, f1) in enumerate(((0, 6), (6, 11))):
                    a_tok = {}
                    for f in range(f0, f1):
                        toks = dense(wg, 512 * f, 4, list(range(KD)), H, th3)
                        sg = []
                        for n_, (b, t) in enumerate(toks):
                            i, tm = tmp()
                            t = sum_pair(tm[:, :, :], b, t, tmp_free[i])
                            t = silu(SG[:, 2 * n_:2 * n_ + 2, :], tm[:, :, :], t, TM2[:, :, :], tm2_free[0])
                            tm2_free[0] = tmp_free[i] = t
                            sg.append(t)
                        toks = dense(wu, 512 * f, 4, list(range(KD)), H, th3)
                        for n_, (b, t) in enumerate(toks):
                            i, tm = tmp()
                            t = sum_pair(tm[:, :, :], b, t, tmp_free[i])
                            t = tt(tm[:, :, :], tm[:, :, :], SG[:, 2 * n_:2 * n_ + 2, :], ALU.mult, t, sg[n_])
                            k = 4 * (f - f0) + 2 * n_
                            t = split_x(tm[:, :, :], ACTS, k, 2, t, acts_free)
                            tmp_free[i] = t
                            a_tok[k] = a_tok[k + 1] = t
                    out_proj(wdn, list(range(4 * f0, 4 * f1)), ACTS, lambda n: a_tok[n], T2,
                             first=(part == 0), last=(part == 1))
                    acts_free = (s_pe, PE.n)
                r = rstd(D, 1e-6)
                for x_tok in residual(T2, gcol["ffnpost"], r, False):
                    pass
            drain()
            if stop == "o_a":
                pass
            last_v = (s_dve, DV.n)
            last_pe = (s_pe, PE.n)
            y = out.rearrange("a (t p) d -> p (a t) d", p=P)
            nout = 0
            for m in range(4):
                for t in range(2):
                    b = take(2)
                    PE.wait(bank_free[b], last_v)
                    for j in range(4):
                        e_ = tr(ps[:, b, j * P:(j + 1) * P], xT[:, 4 * m + j, t * P:(t + 1) * P], inc=(j == 3))
                    d = YN[:, t, 512 * m:512 * m + 512]
                    t_ = act(d, ps[:, b, :], ACT.Copy, e_, last_pe)
                    bank_free[b] = t_
                    nout += 16
                    SP.dma(lambda e, d=d, t=t, m=m: e.dma_start(y[:, t, 512 * m:512 * m + 512], d), s_out,
                           nout, t_)
            SP.wait(t_bv, (s_out, nout))
            return chunks, PE, AC, DV, SP

        chunks, *_ = program([])
        _, PE, AC, DV, SP = program(chunks)
        s_n = sem("s_n")
        block = ctx.enter_context(nc.Block())

        @block.tensor
        def _(e):
            e.wait_ge(s_n, 1)
            PE.play(e)

        @block.vector
        def _(e):
            e.memset(NONES[:, :], -1.0).then_inc(s_n, 1)
            DV.play(e)

        @block.scalar
        def _(e):
            AC.play(e)

        @block.sync
        def _(e):
            SP.play(e)


_INS = ["x", "p", "norm_pre", "norm_post", "w_in_a", "w_out_a", "w_in_b", "q_latent_norm", "w_uq", "w_out_b",
        "kv_norm", "w_dkv", "kv_latent_norm", "w_uk", "w_uv", "w_ple_proj", "w_ple_gate", "w_in_2", "w_out_2",
        "lambda_q1_2", "lambda_k1_2", "lambda_q2_2", "lambda_k2_2", "subln_gain_2", "conv_w_2",
        "conv_norm_gain_2", "rel_bias_2", "w_gate_2", "w_up_2", "w_down_2", "norm_mix_pre_2",
        "norm_mix_post_2", "norm_ffn_pre_2", "norm_ffn_post_2"]


def constants():
    f = np.float32
    i = np.arange(P)
    t = {}
    t["ident"] = np.eye(P, dtype=f)
    t["flip"] = np.eye(P, dtype=f)[::-1]
    t["tri"] = -(i[:, None] >= i[None, :]).astype(f)
    t["ones"] = np.ones((P, P), f)
    perm = np.zeros((P, P), f)
    perm[i ^ 32, i] = 1.0
    t["perm"] = perm
    t["mask"] = (i[:, None] < i[None, :]).astype(f)
    t["negA"] = np.where(i[:, None] >= i[None, :], f(-1e30), f(0))
    t["negB"] = np.where((i[:, None] < 64) & (i[None, :] >= 64), f(-1e30), f(0))
    inv = (f(1.0) / (f(10000.0) ** (np.arange(0, 64, 2, dtype=f) / f(64)))).astype(f)
    ang = np.arange(S, dtype=f)[None, :] * inv[i % 32][:, None]
    t["cos"] = np.cos(ang).astype(f)
    t["sin"] = (np.sin(ang) * np.where(i % 64 < 32, -1.0, 1.0)[:, None]).astype(f)
    cst = np.concatenate([t[n].astype(f) for n in CONST], axis=1)
    d = 255 - np.arange(384)
    n = np.maximum(d, 0)
    nf = np.maximum(n, 16).astype(f)
    large = 16 + (np.log(nf / f(16)) / f(math.log(8.0)) * f(16)).astype(np.int32)
    large = np.minimum(large, 31)
    bucket = np.where(n < 16, n, large)
    oh = np.zeros((33, 384), f)
    oh[bucket, np.arange(384)] = 1.0
    oh[32] = np.where(d < 0, f(-1e30), f(0))
    return np.ascontiguousarray(cst), oh


def kernel(**inputs):
    import concourse.bacc as _bacc
    from concourse.bass_utils import run_bass_kernel_spmd as _run

    nc = _bacc.Bacc("TRN2", target_bir_lowering=False, num_devices=1)
    arrays, aps = {}, {}
    for name in _INS:
        v = np.ascontiguousarray(inputs[name])
        arrays[f"in_{name}"] = v
        aps[name] = nc.dram_tensor(f"in_{name}", v.shape, mybir.dt.from_np(v.dtype), kind="ExternalInput").ap()
    cst, oh = constants()
    arrays["cst"], arrays["oh"] = cst, oh
    c_ap = nc.dram_tensor("cst", cst.shape, F32, kind="ExternalInput").ap()
    o_ap = nc.dram_tensor("oh", oh.shape, F32, kind="ExternalInput").ap()
    y = nc.dram_tensor("out", (1, S, D), F32, kind="ExternalOutput").ap()
    build(nc, aps, c_ap, o_ap, y, STOP)
    r = _run(nc, [arrays], core_ids=[0])
    return r.results[0]["out"]


STOP = None
```

```python
import math
from contextlib import ExitStack

import numpy as np
import concourse.bass as bass
from concourse import mybir

F32 = mybir.dt.float32
F32R = mybir.dt.float32r
BF16 = mybir.dt.bfloat16
ALU = mybir.AluOpType
ACT = mybir.ActivationFunctionType
AX = mybir.AxisListType

P = 128
S = 256
D = 2048
KD = D // P
DFF = 5632
NRAW = 4
NSPL = 4
AHEAD = 4
CH = 1024
CONST = ["ident", "flip", "tri", "ones", "perm", "mask", "cos", "sin", "negA", "negB"]
CW = {"cos": 256, "sin": 256}


class Queue:

    def __init__(self, sem):
        self.sem, self.n, self.ops, self.seen = sem, 0, [], {}

    def wait(self, *tokens):
        for t in tokens:
            if t is None:
                continue
            if isinstance(t, list):
                self.wait(*t)
                continue
            sem, value = t
            if self.seen.get(sem, 0) < value:
                self.seen[sem] = value
                self.ops.append(lambda e, sem=sem, value=value: e.wait_ge(sem, value))

    def do(self, fn, *tokens, inc=True):
        self.wait(*tokens)
        if not inc:
            self.ops.append(fn)
            return None
        self.n += 1
        self.ops.append(lambda e: fn(e).then_inc(self.sem, 1))
        return (self.sem, self.n)

    def dma(self, fn, sem, value, *tokens):
        self.wait(*tokens)
        self.ops.append(lambda e: fn(e).then_inc(sem, 16))
        return (sem, value)

    def play(self, eng):
        for op in self.ops:
            op(eng)


def build(nc, a, cst, onehot, out, stop=None):
    ctx = ExitStack()
    with ctx:
        BASE = 16512
        pos = [BASE]

        def at(name, shape, dt, off):
            return nc.alloc_sbuf_tensor_at(name, shape, dt, offset=off)

        def sb(name, shape, dt=F32):
            n = int(np.prod(shape[1:])) * (2 if dt == BF16 else 4)
            t = at(name, shape, dt, pos[0])
            pos[0] += (n + 31) // 32 * 32
            return t

        xT = sb("xT", [P, KD, S])
        H = sb("H", [P, KD, 2 * S], F32R)
        R1 = pos[0]
        O = at("O", [P, KD, 2 * S], F32R, R1)
        SL = [R1 + 32768 + 18432 * s for s in range(2)]
        qT = [at(f"qT{s}", [P, 4, S], F32, SL[s]) for s in range(2)]
        kT = [at(f"kT{s}", [P, 4, S], F32, SL[s] + 4096) for s in range(2)]
        Vn = [at(f"Vn{s}", [P, 2, 512], F32, SL[s] + 8192) for s in range(2)]
        gT = [at(f"gT{s}", [P, 4, S], F32, SL[s] + 12288) for s in range(2)]
        qR = [at(f"qR{s}", [P, 2, S], F32, SL[s] + 16384) for s in range(2)]
        T = at("T", [P, KD, S], F32, SL[0])
        PP = at("PP", [P, KD, S], F32, SL[1])
        RAWL = at("RAWL", [P, 4, S], F32, SL[1])
        GC = at("GC", [P, 4, S], F32, SL[0] + 12288)
        CT = [at(f"CT{m}", [P, 4, S], F32, SL[1 - m] + 12288 * (1 - m)) for m in range(2)]
        ACTS = at("ACTS", [P, 24, 2 * S], F32R, R1)
        T2 = at("T2", [P, KD, S], F32, R1 + 49152)
        SG = at("SG", [P, 4, S], F32, R1 + 65536)
        XN = at("XN", [P, 2, D], F32, SL[0])
        YN = at("YN", [P, 2, D], F32, R1)
        GN = at("GN", [P, 2, P], F32, SL[1])
        OH = at("OH", [32, 384], F32, SL[1] + 1024)
        RB = at("RB", [32, 8], F32, SL[1] + 2560)
        MR = at("MR", [1, 384], F32, SL[1] + 2592)
        BV = at("BV", [8, 384], F32, SL[1] + 4128)
        LM = at("LM", [1, 4, 64], F32, SL[1] + 5664)
        LP = at("LP", [1, 2, 64], F32, SL[1] + 6688)
        LS = at("LS", [1, 8], F32, SL[1] + 7200)
        NG = at("NG", [P, 2, P], F32, SL[1] + 7232)
        pos[0] = R1 + 69632
        L1 = pos[0]
        CKV = sb("CKV", [P, 4, 2 * S], F32R)
        CQ = sb("CQ", [P, 4, 2 * S], F32R)
        RT = at("RT", [P, 8, S], F32, L1)
        KR = sb("KR", [P, S])
        PN = sb("PN", [P, 2, S])
        RAW = sb("RAW", [P, NRAW, CH])
        WH = sb("WH", [P, NSPL, CH], F32R)
        WL = sb("WL", [P, NSPL, CH], F32R)
        C = {n: sb("c_" + n, [P, CW.get(n, P)]) for n in CONST[:8]}
        identb = sb("identb", [P, P], BF16)
        negb = [sb(f"negb{i}", [P, P], BF16) for i in range(2)]
        GAIN = sb("GAIN", [P, 256])
        NLAM = sb("NLAM", [P, 3])
        TMP = [sb(f"TMP{i}", [P, 2, S]) for i in range(2)]
        SQ = sb("SQ", [P, 2, S])
        ACC = sb("ACC", [P, 2, S])
        RSX = sb("RSX", [P, S])
        RS = sb("RS", [P, S])
        RC = sb("RC", [P, 2])
        F1 = sb("F1", [P, 2, 384])
        F2 = sb("F2", [P, 2, 384])
        RV, RW = SQ[:, 0, :], SQ[:, 1, :]
        SM = sb("SM", [P, 16])
        NONES = sb("NONES", [P, P])
        C["negones"] = NONES[:, :]
        print('free', 229344 - pos[0])
        if pos[0] > 229344:
            raise ValueError(f"SBUF over by {pos[0] - 229344}")

        ps = ctx.enter_context(nc.psum_tensor("ps", [P, 8, 512], F32))
        bvd = nc.dram_tensor("bvd", (8, 384), F32, kind="Internal").ap()

        def sem(name):
            return ctx.enter_context(nc.semaphore(name))

        s_pe, s_act, s_dve = sem("s_pe"), sem("s_act"), sem("s_dve")
        s_raw = [sem(f"s_raw{i}") for i in range(NRAW)]
        s_in = [sem(f"s_in{i}") for i in range(16)]
        s_out = sem("s_out")

        def program(chunks_known):
            PE, AC, DV, SP, GP = Queue(s_pe), Queue(s_act), Queue(s_dve), Queue(None), Queue(None)
            chunks = []

            def V(fn, *t):
                return DV.do(fn, *t)

            def A(fn, *t):
                return AC.do(fn, *t)

            table = [None]

            def act(o, i, f, *t, **kw):
                need = 1 if f in (ACT.Exp, ACT.Ln) else 2 if f in (ACT.Silu, ACT.Sigmoid) else table[0]
                if need == 1 and table[0] != 1:
                    AC.do(lambda e: e.preload_act_table_set("natural_log_exp_and_others"), inc=False)
                table[0] = need
                return A(lambda e: e.activation(o, i, f, **kw), *t)

            def tt(o, x, y, op, *t):
                return V(lambda e: e.tensor_tensor(o, x, y, op), *t)

            def ts(o, x, s1, s2, op0, op1, *t):
                if op1 is None:
                    return V(lambda e: e.tensor_scalar(o, x, s1, None, op0), *t)
                return V(lambda e: e.tensor_scalar(o, x, s1, s2, op0, op1), *t)

            def stt(o, x, s, y, op0, op1, *t):
                return V(lambda e: e.scalar_tensor_tensor(out=o, in0=x, scalar=s, in1=y, op0=op0, op1=op1), *t)

            def mm(o, l, r, start=False, *t, inc=False):
                return PE.do(lambda e: e.matmul(o, l, r, start=start, stop=True, skip_group_check=True), *t, inc=inc)

            def tr(o, i, *t, inc=False):
                idn = C["ident"][:, :] if i.shape[0] == P else C["ident"][0:i.shape[0], 0:i.shape[0]]
                return PE.do(lambda e: e.transpose(o, i, idn), *t, inc=inc)

            small = [0]

            def load(dst, src, q=None, *t):
                i = small[0]
                small[0] += 1
                return (q or GP).dma(lambda e: e.dma_start(dst, src), s_in[i], 16, *t)

            raw_count = [0] * NRAW
            raw_tok, raw_free = {}, {}
            spl_tok, spl_free = {}, {}
            loaded, split = [0], [0]

            def load_chunk():
                i = loaded[0]
                if i >= len(chunks_known):
                    return
                loaded[0] += 1
                slot = i % NRAW
                SP.wait(raw_free.get(i - NRAW))
                for off, n, src in chunks_known[i][0]:
                    dst = RAW[:, slot, off:off + n]
                    raw_count[slot] += 16
                    if len(src.shape) == 3:
                        dst = dst.rearrange("p (a b) -> p a b", a=src.shape[1])
                    raw_tok[i] = SP.dma(lambda e, dst=dst, src=src: e.dma_start(dst, src),
                                        s_raw[slot], raw_count[slot])

            def split_chunk():
                i = split[0]
                if i >= len(chunks_known):
                    return
                split[0] += 1
                r, w, n = i % NRAW, i % NSPL, chunks_known[i][1]
                raw, hi, lo = RAW[:, r, 0:n], WH[:, w, 0:n], WL[:, w, 0:n]
                th = act(hi, raw, ACT.Copy, raw_tok[i], spl_free.get(i - NSPL))
                spl_tok[i] = tt(lo, raw, hi.bitcast(F32), ALU.subtract, th)
                raw_free[i] = [th, spl_tok[i]]
                load_chunk()

            def next_chunk(parts, n):
                i = len(chunks)
                chunks.append((parts, n))
                if chunks_known:
                    while split[0] <= min(i + AHEAD - 1, len(chunks_known) - 1):
                        split_chunk()
                return i

            bg = []

            fg = []

            def step(q):
                while q:
                    try:
                        next(q[0])
                        return
                    except StopIteration:
                        q.pop(0)

            def bgstep():
                step(bg)

            def drain():
                while bg:
                    step(bg)

            def at_once(q, gen, n=0):
                for _ in range(n):
                    next(gen)
                q.append(gen)

            def need(d, n):
                while n not in d:
                    step(fg)
                    if n not in d:
                        step(bg)
                return d[n]

            bank_free = {b: None for b in range(8)}
            ring = [0]

            def take(n):
                b = ring[0]
                ring[0] = (b + n) % 6
                return b

            def dense(src, c0, nt, kts, xs, xt, per=2, natural=False, view=None):
                nk = len(kts)
                b0 = take(2 if natural else (nt + 1) // 2 * 2)
                w = nt * P
                toks = []
                for ci in range(0, nk, per):
                    ks = kts[ci:ci + per]
                    if view:
                        parts = [p for j, k in enumerate(ks) for p in view(j, k)]
                    else:
                        parts = [(0, len(ks) * w, src[ks[0] * P:(ks[-1] + 1) * P, c0:c0 + w]
                                  .rearrange("(c p) n -> p c n", p=P))]
                    i = next_chunk(parts, len(ks) * w)
                    if chunks_known:
                        PE.wait(spl_tok[i])
                    hi = WH[:, i % NSPL, 0:len(ks) * w].rearrange("p (c n) -> p c n", n=w)
                    lo = WL[:, i % NSPL, 0:len(ks) * w].rearrange("p (c n) -> p c n", n=w)
                    last_chunk = ci + per >= nk
                    if natural:
                        if ci == 0:
                            PE.wait(bank_free[b0], bank_free[b0 + 1])
                        for j, k in enumerate(ks):
                            n = ci + j
                            PE.wait(xt(n))
                            for t in range(2):
                                xh = xs[:, n, t * P:(t + 1) * P]
                                xl = xs[:, n, S + t * P:S + (t + 1) * P]
                                o = ps[:, b0 + t, :]
                                mm(o, xh, hi[:, j, :], n == 0)
                                mm(o, xh, lo[:, j, :])
                                end = mm(o, xl, hi[:, j, :], inc=(t == 1 and j == len(ks) - 1))
                        if last_chunk:
                            toks.append((b0, end))
                    else:
                        for t in range(nt):
                            b = (b0 + t) % 6
                            if ci == 0:
                                PE.wait(bank_free[b])
                            for j, k in enumerate(ks):
                                n = ci + j
                                PE.wait(xt(n))
                                wh, wl = hi[:, j, t * P:(t + 1) * P], lo[:, j, t * P:(t + 1) * P]
                                mm(ps[:, b, :], wh, xs[:, n, :], n == 0)
                                fin = j == len(ks) - 1 and (t == nt - 1 or (last_chunk and t % 2 == 1))
                                end = mm(ps[:, b, S:2 * S], wl, xs[:, n, 0:S], inc=fin)
                            if last_chunk and (t % 2 == 1 or t == nt - 1):
                                toks.append((b - t % 2, end))
                    spl_free[i] = end
                    step(fg)
                    step(bg)
                return toks

            def halves(b, n=2):
                return ps[:, b:b + n, 0:S], ps[:, b:b + n, S:2 * S]

            def release(b, tok, n=2):
                for i in range(n):
                    bank_free[b + i] = tok

            def sum_pair(o, b, tok, *t, n=2):
                x, y = halves(b, n)
                r = act(o, y, ACT.Copy, tok, *t)
                r = tt(o, x, o, ALU.add, r)
                release(b, r, n)
                return r

            tmp_free = [None, None]
            tmp_at = [0]

            def tmp():
                i = tmp_at[0]
                tmp_at[0] = 1 - i
                return i, TMP[i]

            def bc(ap, n=2):
                return ap.unsqueeze(1).broadcast_to([P, n, ap.shape[-1]])

            def split_x(src, dst, k0, n, dep, *war):
                th = act(dst[:, k0:k0 + n, 0:S], src, ACT.Copy, dep, *war)
                return tt(dst[:, k0:k0 + n, S:2 * S], src, dst[:, k0:k0 + n, 0:S].bitcast(F32),
                          ALU.subtract, th)

            st = {"first": True, "acc": None, "accfree": None, "sq": None, "rs": None}

            def sq_add(src, dep):
                if st["first"]:
                    st["acc"] = act(ACC[:, :, :], src, ACT.Square, dep, st["accfree"])
                    st["first"] = False
                    return st["acc"]
                t = act(SQ[:, :, :], src, ACT.Square, dep, st["sq"])
                st["acc"] = st["sq"] = tt(ACC[:, :, :], ACC[:, :, :], SQ[:, :, :], ALU.add, t, st["acc"])
                return t

            def later(n, gen):
                for _ in range(n):
                    yield
                yield from gen

            def rstd(dim, eps, rs, done, cols=False):
                PE.wait(bank_free[6], st["acc"])
                mm(ps[:, 6, 0:S], C["ones"][:, :], ACC[:, 0, :], True)
                t = mm(ps[:, 6, 0:S], C["ones"][:, :], ACC[:, 1, :], inc=True)
                st["accfree"], st["first"] = t, True
                t = ts(RV, ps[:, 6, 0:S], 1.0 / dim, eps, ALU.mult, ALU.add, t)
                bank_free[6] = t
                st["sq"] = t = rsqrt(rs[:, :], RV, RW, t)
                if cols:
                    yield
                    yield
                    PE.wait(bank_free[7], t)
                    tr(ps[:, 7, 0:P], rs[:, 0:P])
                    t2 = tr(ps[:, 7, P:S], rs[:, P:S], inc=True)
                    t2 = V(lambda e: e.tensor_copy(RC[:, :], ps[:, 7, 0:S:P]), t2)
                    bank_free[7] = t2
                    t = [t, t2]
                done[0] = t

            def rstd_now(dim, eps, rs=None):
                drain()
                d = {}
                for _ in rstd(dim, eps, rs or RS, d):
                    pass
                return d[0]

            def rsqrt(o, v, w, dep):
                t = act(w, v, ACT.Ln, dep)
                t = act(o, w, ACT.Exp, t, scale=-0.5)
                t = stt(w, o, -0.5, o, ALU.mult, ALU.mult, t)
                t = tt(w, w, v, ALU.mult, t)
                return stt(o, w, 1.5, o, ALU.add, ALU.mult, t)

            def norm_to(src, g0, dst, n, r, *war):
                toks = {}
                for c in range(0, n, 2):
                    i, tm = tmp()
                    for j in range(2):
                        t = stt(tm[:, j, :], src[:, c + j, :], GAIN[:, g0 + c + j:g0 + c + j + 1], RS[:, :],
                                ALU.mult, ALU.mult, r, tmp_free[i])
                    t = split_x(tm[:, :, :], dst, c, 2, t, *war)
                    tmp_free[i] = t
                    toks[c] = toks[c + 1] = t
                return toks

            def gained(c, g0, dst, toks, dep, *war):
                for j in range(2):
                    g = GAIN[:, g0 + c + j:g0 + c + j + 1]
                    th = act(dst[:, c + j, 0:S], xT[:, c + j, :], ACT.Copy, dep, *war, scale=g)
                for j in range(2):
                    g = GAIN[:, g0 + c + j:g0 + c + j + 1]
                    t = stt(dst[:, c + j, S:2 * S], xT[:, c + j, :], g, dst[:, c + j, 0:S].bitcast(F32),
                            ALU.mult, ALU.subtract, th)
                toks[c] = toks[c + 1] = t

            off = 0
            cl = []
            for n in CONST:
                w = CW.get(n, P)
                if n in CONST[:8]:
                    cl.append((C[n][:, :], off, w))
                else:
                    cl.append((NG[:, CONST.index(n) - 8, :], off, w))
                off += w
            t_ident = load(cl[0][0], cst[:, 0:P], SP)
            xr = a["x"].rearrange("a (t p) d -> p (a t) d", p=P)
            t_x = []
            for m in range(4):
                t_x.append(load(XN[:, :, 512 * m:512 * m + 512], xr[:, :, 512 * m:512 * m + 512], SP))
                if chunks_known:
                    load_chunk()
            gi = [0]
            gcol, load_rows = {}, []

            def grow(name, src, rows):
                if gi[0] < P < gi[0] + rows:
                    gi[0] = P
                r = gi[0]
                gcol[name] = r
                gi[0] += rows
                load_rows.append((GN[r % P:r % P + rows, r // P, 0:src.shape[-1]], src))

            r16 = lambda v: v.rearrange("(c p) -> c p", p=P)
            for l in range(2):
                grow(f"pre{l}", r16(a["norm_pre"][l]), 16)
            t_g0 = load(load_rows[0][0], load_rows[0][1], AC)
            grow("mixpre", r16(a["norm_mix_pre_2"][0]), 16)
            for l in range(2):
                grow(f"post{l}", r16(a["norm_post"][l]), 16)
            grow("kv", r16(a["kv_norm"]), 16)
            grow("mixpost", r16(a["norm_mix_post_2"][0]), 16)
            grow("ffnpre", r16(a["norm_ffn_pre_2"][0]), 16)
            grow("ffnpost", r16(a["norm_ffn_post_2"][0]), 16)
            grow("ckv", r16(a["kv_latent_norm"]), 4)
            grow("cq", r16(a["q_latent_norm"][0]), 4)
            for j in range(3):
                grow(f"cw{j}", r16(a["conv_w_2"][0, j]), 8)
            grow("cn", r16(a["conv_norm_gain_2"][0]), 8)
            grow("sub", a["subln_gain_2"], 1)
            i = small[0]
            small[0] += 1
            for n_, (dst, o_, w) in enumerate(cl[1:]):
                t_cst = GP.dma(lambda e, dst=dst, o_=o_, w=w: e.dma_start(dst, cst[:, o_:o_ + w]), s_in[i],
                               16 * (n_ + 1))
            t_p = load(PN[:, :, :], a["p"][0, 0].rearrange("(t p) d -> p t d", p=P))
            i = small[0]
            small[0] += 1
            for n_, (dst, src) in enumerate(load_rows[1:]):
                t_g = GP.dma(lambda e, dst=dst, src=src: e.dma_start(dst, src), s_in[i], 16 * (n_ + 1))
            nrow2 = gi[0] - P
            t_oh = load(OH[:, :], onehot[0:32, :])
            t_mr = load(MR[:, :], onehot[32:33, :])
            t_rb = load(RB[:, :], a["rel_bias_2"])
            i = small[0]
            small[0] += 1
            for n_, nm in enumerate(["q1", "k1", "q2", "k2"]):
                t_lm = GP.dma(lambda e, n_=n_, nm=nm: e.dma_start(LM[:, n_, :], a[f"lambda_{nm}_2"]), s_in[i],
                              16 * (n_ + 1))
            PE.wait(t_ident, t_g0)
            t = tr(ps[:, 7, 0:16], GN[0:16, 0, :], inc=True)
            t_g0 = V(lambda e: e.tensor_copy(GAIN[:, 0:16], ps[:, 7, 0:16]), t)
            bank_free[7] = t_g0
            t_h = {}

            def x_in():
                for c in range(0, KD, 2):
                    b = 4 + c // 2 % 2
                    PE.wait(bank_free[b])
                    for j in range(2):
                        for t in range(2):
                            e_ = tr(ps[:, b, j * S + t * P:j * S + (t + 1) * P],
                                    XN[:, t, (c + j) * P:(c + j + 1) * P], t_x[c // 4], inc=(j == 1 and t == 1))
                    t_v = V(lambda e, b=b, c=c: e.tensor_copy(
                        xT[:, c:c + 2, :], ps[:, b, :].rearrange("p (j s) -> p j s", j=2)), e_)
                    bank_free[b] = t_v
                    gained(c, gcol["pre0"], H, t_h, [t_v, t_g0])
                    yield
                for c in range(0, KD, 2):
                    sq_add(xT[:, c:c + 2, :], None)
                    if c % 4 == 2:
                        yield
                t_h["sq"] = True

            at_once(fg, x_in(), 2)
            r_a, late = {}, {}

            def p_split(t_p, *war):
                PE.wait(bank_free[7], t_p, *war)
                for k in range(2):
                    for t in range(2):
                        e_ = tr(ps[:, 7, k * S + t * P:k * S + (t + 1) * P], PN[:, t, k * P:(k + 1) * P],
                                inc=(k == 1 and t == 1))
                i, tm = tmp()
                t = V(lambda e: e.tensor_copy(tm[:, :, :], ps[:, 7, :].rearrange("p (k s) -> p k s", k=2)),
                      e_, tmp_free[i])
                bank_free[7] = t
                t = split_x(tm[:, :, :], CQ, 0, 2, t, *war)
                tmp_free[i] = t
                return [e_, t]

            def setup_late():
                yield from rstd_first()
                PE.wait(bank_free[7], t_g)
                tr(ps[:, 7, 0:P], GN[:, 0, :])
                t = tr(ps[:, 7, P:P + nrow2], GN[0:nrow2, 1, :], inc=True)
                t = V(lambda e: e.tensor_copy(GAIN[:, 16:P + nrow2], ps[:, 7, 16:P + nrow2]), t)
                bank_free[7] = t
                s0 = gcol["sub"]
                ts(GAIN[:, s0:s0 + 1], GAIN[:, s0:s0 + 1], 0.8, None, ALU.mult, None, t)
                yield
                V(lambda e: e.tensor_copy(identb[:, :], C["ident"][:, :]), t_cst)
                for j in range(2):
                    V(lambda e, j=j: e.tensor_copy(negb[j][:, :], NG[:, j, :]))
                yield
                PE.wait(bank_free[6], t_oh, t_rb, t_mr)
                mm(ps[0:8, 6, 0:384], RB[:, :], OH[:, :], True)
                t = mm(ps[0:8, 6, 0:384], C["ones"][0:1, 0:8], MR[:, :], inc=True)
                t = V(lambda e: e.tensor_copy(BV[:, :], ps[0:8, 6, 0:384]), t)
                bank_free[6] = t
                late["bv"] = load(bvd, BV[:, :], GP, t)
                yield
                t = tt(LP[:, :, :], LM[:, 0:4:2, :], LM[:, 1:4:2, :], ALU.mult, t_lm)
                t = V(lambda e: e.tensor_reduce(LS[:, 0:2], LP[:, :, :], AX.X, ALU.add), t)
                t = act(LS[:, 2:4], LS[:, 0:2], ACT.Exp, t)
                t = tt(LS[:, 4:5], LS[:, 3:4], LS[:, 2:3], ALU.subtract, t)
                t = ts(LS[:, 4:5], LS[:, 4:5], -(0.8 - 0.6 * math.exp(0.0)), None, ALU.add, None, t)
                t = stt(LS[:, 7:8], LS[:, 4:5], -1.0, LS[:, 4:5], ALU.mult, ALU.max, t)
                t = ts(LS[:, 7:8], LS[:, 7:8], 1.0, None, ALU.max, None, t)
                t = V(lambda e: e.reciprocal(LS[:, 5:6], LS[:, 7:8]), t)
                t = tt(LS[:, 4:5], LS[:, 4:5], LS[:, 5:6], ALU.mult, t)
                t = stt(LS[:, 6:7], LS[:, 5:6], 1e-5, LS[:, 5:6], ALU.mult, ALU.mult, t)
                yield
                yield
                PE.wait(bank_free[7], t)
                t = mm(ps[:, 7, 0:3], C["ones"][0:1, :], LS[:, 4:7], True, inc=True)
                t = V(lambda e: e.tensor_copy(NLAM[:, :], ps[:, 7, 0:3]), t)
                bank_free[7] = t
                late["t"] = t
                yield
                late["p"] = p_split(t_p)

            def rstd_first():
                while "sq" not in t_h:
                    yield
                yield
                PE.wait(t_cst)
                yield from rstd(D, 1e-6, RSX, r_a, True)

            bg.append(setup_late())
            OB, o_war = [O], [None]
            o_tok = {}
            slot_pe = [None, None]

            f_free = {"F1": None, "F2": None}

            def pv(slot, vi, nb, w_tok, fin):
                for j in range(nb):
                    PE.wait(w_tok, fin)
                    vc = (vi + j) * P
                    mm(ps[:, 6 + j, 0:S], Vn[slot][:, 0, vc:vc + P], F1[:, j, 0:S], True)
                    t = mm(ps[:, 6 + j, P:S], Vn[slot][:, 1, vc:vc + P], F1[:, j, S:384], inc=(j == nb - 1))
                f_free["F1"] = t
                slot_pe[slot] = t
                return t

            def gate_out(slot, gi_, h0, t, g_tok):
                i, tm = tmp()
                t = tt(tm[:, :, :], ps[:, 6:8, 0:S], gT[slot][:, gi_:gi_ + 2, :], ALU.mult, t, g_tok, tmp_free[i])
                release(6, t)
                t = split_x(tm[:, :, :], OB[0], h0, 2, t, o_war[0])
                tmp_free[i] = t
                o_tok[h0] = o_tok[h0 + 1] = t

            def attn_a(slot, h0, i0, toks):
                PE.wait(bank_free[6], bank_free[7], toks[0:2])
                for j in range(2):
                    q, k = qT[slot][:, i0 + j, :], kT[slot][:, i0 + j, :]
                    mm(ps[:, 6 + j, 0:S], k[:, 0:P], q, True)
                    t = mm(ps[:, 6 + j, S:384], k[:, P:S], q[:, P:S], inc=(j == 1))
                yield
                z = ps[:, 6:8, 0:384]
                t = act(F1[:, :, :], z, ACT.Abs, t, f_free["F1"])
                t = act(F1[:, :, :], F1[:, :, :], ACT.Exp, t, scale=-1.0)
                t = act(F1[:, :, :], F1[:, :, :], ACT.Ln, t, bias=1.0)
                yield
                t = stt(F2[:, :, :], z, 0.0, F1[:, :, :], ALU.max, ALU.add, t, f_free["F2"])
                for c in (0, S):
                    d = F2[:, :, c:c + P]
                    t = tt(d, d, bc(C["mask"][:, :]), ALU.mult, t)
                yield
                yield
                PE.wait(t)
                for j in range(2):
                    b = 6 + j
                    mm(ps[:, b, 0:384], C["tri"][:, :], F2[:, j, :])
                    mm(ps[:, b, P:S], C["negones"], F2[:, j, S:384])
                    for c in (0, S):
                        t = mm(ps[:, b, c:c + P], identb[:, :], negb[0][:, :], inc=(j == 1 and c == S))
                f_free["F2"] = t
                yield
                t = act(F1[:, :, :], z, ACT.Exp, t)
                yield
                yield
                t = pv(slot, i0, 2, t, toks[:-1])
                yield
                while not toks[-1]:
                    yield
                gate_out(slot, i0, h0, t, toks)

            def softmax(b0, n, scale, t, lam=None):
                V(lambda e: e.tensor_reduce(SM[:, 0:n], ps[:, b0:b0 + n, 0:P], AX.X, ALU.max), t, f_free["SM"])
                t = V(lambda e: e.tensor_reduce(SM[:, 2:2 + n], ps[:, b0:b0 + n, P:384], AX.X, ALU.max))
                t = ts(SM[:, 4:8], SM[:, 0:4], -scale, None, ALU.mult, None, t)
                for j in range(n):
                    for q in range(2):
                        c0, c1 = (0, P) if q == 0 else (P, 384)
                        cc = 2 * q + j
                        tn = A(lambda e, j=j, c0=c0, c1=c1, cc=cc: e.activation(
                            F2[:, j, c0:c1], ps[:, b0 + j, c0:c1], ACT.Exp, bias=SM[:, 4 + cc:5 + cc],
                            scale=scale, accum_out=SM[:, 8 + cc:9 + cc]), t, f_free["F2"])
                t = V(lambda e: e.reciprocal(SM[:, 12:16], SM[:, 8:12]), tn)
                return t

            f_free["SM"] = None

            def turn(j, t):
                PE.wait(t)
                tr(ps[:, 6 + j, 0:P], F2[:, j, 0:P])
                tr(ps[:, 6 + j, P:S], F2[:, j, P:S])
                return tr(ps[:, 6 + j, S:384], F2[:, j, S:384], inc=True)

            def attn_b(slot, h0, i0, toks, kr_tok):
                PE.wait(bank_free[6], bank_free[7], toks[0:4], kr_tok)
                for j in range(2):
                    b, i = 6 + j, i0 + j
                    q, k = qT[slot][:, i, :], kT[slot][:, i, :]
                    r0 = 64 * (i % 2)
                    qr, kr = qR[slot][r0:r0 + 64, i // 2, :], KR[r0:r0 + 64, :]
                    mm(ps[:, b, 0:P], q[:, 0:P], k[:, 0:P], True)
                    mm(ps[:, b, P:384], q[:, P:S], k)
                    mm(ps[:, b, 0:P], qr[:, 0:P], kr[:, 0:P])
                    mm(ps[:, b, P:384], qr[:, P:S], kr)
                    mm(ps[:, b, 0:P], identb[:, :], negb[1][:, :])
                    t = mm(ps[:, b, S:384], identb[:, :], negb[1][:, :], inc=(j == 1))
                yield
                t = softmax(6, 2, 192 ** -0.5, t)
                for j in range(2):
                    for q in range(2):
                        c0, c1 = (0, P) if q == 0 else (P, 384)
                        cc = 12 + 2 * q + j
                        t = ts(F2[:, j, c0:c1], F2[:, j, c0:c1], SM[:, cc:cc + 1], None, ALU.mult, None, t)
                yield
                yield
                turn(0, t)
                t = turn(1, t)
                f_free["F2"] = t
                yield
                t = act(F1[:, :, :], ps[:, 6:8, 0:384], ACT.Copy, t, f_free["F1"])
                yield
                t = pv(slot, i0, 2, t, toks[:-1])
                yield
                while not toks[-1]:
                    yield
                gate_out(slot, i0, h0, t, toks)

            def attn_c(slot, h, i, toks, rt_tok):
                PE.wait(bank_free[6], bank_free[7], toks, rt_tok)
                for j in range(2):
                    b, r0 = 6 + j, 64 * j
                    q, k = qT[slot][r0:r0 + 64, i, :], kT[slot][r0:r0 + 64, i, :]
                    mm(ps[:, b, 0:P], q[:, 0:P], k[:, 0:P], True)
                    mm(ps[:, b, P:384], q[:, P:S], k)
                    mm(ps[:, b, 0:P], C["flip"][:, :], RT[:, h, P:S])
                    t = mm(ps[:, b, P:384], C["flip"][:, :], RT[:, h, :], inc=(j == 1))
                yield
                t = softmax(6, 2, 1.0, t)
                t2 = ts(SM[:, 0:2], SM[:, 13:16:2], NLAM[:, 0:1], None, ALU.mult, None, t)
                t2 = ts(SM[:, 2:4], SM[:, 12:16:2], NLAM[:, 1:2], None, ALU.mult, None, t2)
                for q in range(2):
                    c0, c1 = (0, P) if q == 0 else (P, 384)
                    t = ts(F2[:, 0, c0:c1], F2[:, 0, c0:c1], SM[:, 2 + q:3 + q], None, ALU.mult,
                           None, t2)
                for q in range(2):
                    c0, c1 = (0, P) if q == 0 else (P, 384)
                    t = stt(F2[:, 0, c0:c1], F2[:, 1, c0:c1], SM[:, q:q + 1], F2[:, 0, c0:c1],
                            ALU.mult, ALU.add, t)
                yield
                yield
                yield
                t = turn(0, t)
                f_free["F2"] = t
                yield
                t = act(F1[:, 0, :], ps[:, 6, 0:384], ACT.Copy, t, f_free["F1"])
                yield
                t = pv(slot, i, 1, t, toks)
                yield
                av, sq, vv, ww = F2[:, 1, 0:S], F2[:, 0, 0:S], F1[:, 0, 0:S], F1[:, 1, 0:S]
                t = V(lambda e: e.tensor_copy(av, ps[:, 6, 0:S]), t)
                release(6, t, 1)
                t = tt(sq, av, av, ALU.mult, t)
                yield
                t = mm(ps[:, 7, 0:S], C["ones"][:, :], sq, True, t, inc=True)
                yield
                t = ts(vv, ps[:, 7, 0:S], 1.0 / P, NLAM[:, 2:3], ALU.mult, ALU.add, t)
                release(7, t, 1)
                t = ts(vv, vv, 2.0 ** -63, None, ALU.max, None, t)
                t = rsqrt(sq, vv, ww, t)
                s_ = gcol["sub"]
                t = stt(av, av, GAIN[:, s_:s_ + 1], sq, ALU.mult, ALU.mult, t)
                th = act(O[:, h, 0:S], av, ACT.Copy, t)
                t = tt(O[:, h, S:2 * S], av, O[:, h, 0:S].bitcast(F32), ALU.subtract, th)
                f_free["F1"] = f_free["F2"] = t
                o_tok[h] = t

            def proj(src, c0, xs, xt, dst, nk=KD, scale=1.0, natural=False, free=None, wk=2, view=None, nt=4,
                     r=None, silu=False):
                toks = dense(src, c0, nt, list(range(nk)), xs, xt, natural=natural, view=view, per=wk)
                if natural:
                    b, t = toks[0]
                    if r is None:
                        t = act(dst, ps[:, b:b + 2, :], ACT.Copy, t, free)
                    else:
                        for j in range(2):
                            t = act(dst[:, j, :], ps[:, b + j, :], ACT.Copy, t, need(r, 0), free,
                                    scale=RC[:, j:j + 1])
                    release(b, t)
                    return t
                return finish(toks, dst, scale, free, r, silu)

            def finish(toks, dst, scale=1.0, free=None, r=None, silu=False):
                ds = [dst[:, 2 * n_:2 * n_ + 2, :] for n_ in range(len(toks))]
                outs = [sum_pair(d, b, t, free) for d, (b, t) in zip(ds, toks)]
                if r is not None:
                    outs = [stt(d, d, scale, bc(RSX[:, :]), ALU.mult, ALU.mult, need(r, 0), t)
                            for d, t in zip(ds, outs)]
                if silu:
                    outs = [act(d, d, ACT.Silu, t) for d, t in zip(ds, outs)]
                return outs

            def summed(toks, r=None):
                outs = []
                for b, t in toks:
                    i, tm = tmp()
                    outs.append((i, tm[:, :, :], sum_pair(tm[:, :, :], b, t, tmp_free[i])))
                if r is not None:
                    outs = [(i, tm, stt(tm, tm, 1.0, bc(RSX[:, :]), ALU.mult, ALU.mult, need(r, 0), t))
                            for i, tm, t in outs]
                return outs

            def out_proj(src, kts, xs, xt, dst, first=True, last=True, free=None):
                for m in range(4):
                    toks = dense(src, 512 * m, 4, kts, xs, xt)
                    if first:
                        outs = finish(toks, dst[:, 4 * m:4 * m + 4, :], free=free)
                    else:
                        outs = []
                        for n_, (i, tm, t) in enumerate(summed(toks)):
                            d = dst[:, 4 * m + 2 * n_:4 * m + 2 * n_ + 2, :]
                            tmp_free[i] = t = tt(d, d, tm, ALU.add, t)
                            outs.append(t)
                    if last:
                        for n_, t in enumerate(outs):
                            sq_add(dst[:, 4 * m + 2 * n_:4 * m + 2 * n_ + 2, :], t)

            def residual(src, g0, r, toks, after):
                for c in range(0, KD, 2):
                    i, tm = tmp()
                    for j in range(2):
                        t = stt(tm[:, j, :], src[:, c + j, :], GAIN[:, g0 + c + j:g0 + c + j + 1], RS[:, :],
                                ALU.mult, ALU.mult, r, tmp_free[i])
                    t = tt(xT[:, c:c + 2, :], xT[:, c:c + 2, :], tm[:, :, :], ALU.add, t, st.get("xr"))
                    tmp_free[i] = t
                    after(c, t)
                    yield

            def mixer_tail(l, w_out, wpp, wpg, then):
                out_proj(w_out, list(range(KD)), OB[0], lambda n: need(o_tok, n), T, free=[t_v_last[0]])
                pp_tok, x_tok = [], {}
                o_dead = (s_pe, PE.n)

                def pp(m):
                    toks = dense(wpp, 512 * m, 4, [0, 1], CQ, lambda n: need(late, "p")[1])
                    pp_tok.extend(finish(toks, PP[:, 4 * m:4 * m + 4, :], free=slot_pe[1]))

                def split_again(c, t):
                    t = split_x(xT[:, c:c + 2, :], O, c, 2, t, o_dead)
                    x_tok[c] = x_tok[c + 1] = t

                pp(0)
                pp(1)
                r = rstd_now(D, 1e-6)
                at_once(fg, residual(T, gcol[f"post{l}"], r, None, split_again), 1)
                pp(2)
                pp(3)
                h_tok = {}
                for m in range(4):
                    toks = dense(wpg, 512 * m, 4, list(range(KD)), O, lambda n: need(x_tok, n))
                    outs = summed(toks)
                    outs = [(i, tm, act(tm, tm, ACT.Sigmoid, t)) for i, tm, t in outs]
                    cs = [4 * m, 4 * m + 2]
                    outs = [(i, tm, tt(tm, tm, PP[:, c:c + 2, :], ALU.mult, t, pp_tok[c // 2]))
                            for c, (i, tm, t) in zip(cs, outs)]
                    for c, (i, tm, t) in zip(cs, outs):
                        t = tt(xT[:, c:c + 2, :], xT[:, c:c + 2, :], tm, ALU.add, t)
                        tmp_free[i] = t
                        then(c, h_tok, t, o_dead)
                        st["xr"] = sq_add(xT[:, c:c + 2, :], t)
                return h_tok, (s_pe, PE.n)

            t_v_last = [None]
            w = a["w_in_a"][0]
            th_ = lambda n: need(t_h, n)
            qs = 128 ** -0.5
            for j in range(4):
                s = j % 2
                if j >= 2:
                    need(o_tok, 4 * (j - 2) + 3)
                fr = [slot_pe[s]]
                if j == 1:
                    need(late, "t")
                    fr = [late["t"], late["bv"]]
                tq = proj(w, 512 * j, H, th_, qT[s], scale=qs, free=fr, r=r_a)
                tk = proj(w, D + 512 * j, H, th_, kT[s], free=fr, r=r_a)
                tv = proj(w, 2 * D + 512 * j, H, th_, Vn[s][:, :, :], natural=True, free=fr, r=r_a)
                tg = []
                for i0 in (0, 2):
                    bg.append(attn_a(s, 4 * j + i0, i0, [tq, tk, tv, tg]))
                tg += proj(w, 3 * D + 512 * j, H, th_, gT[s], free=fr, r=r_a, silu=True)
            h_free = (s_pe, PE.n)
            pn_free = need(late, "p")[0]
            t_kv, dead = mixer_tail(0, a["w_out_a"][0], a["w_ple_proj"][0], a["w_ple_gate"][0],
                                    lambda c, toks, t, w_: gained(c, gcol["kv"], H, toks, t, h_free))
            if stop != "a":
                t_p1 = load(PN[:, :, :], a["p"][1, 0].rearrange("(t p) d -> p t d", p=P), SP, pn_free)
                r_b, t_hb, kr = {}, {}, {}
                bg.append(later(2, rstd(D, 1e-6, RSX, r_b, True)))

                def make_hb():
                    for c in range(0, KD, 2):
                        gained(c, gcol["pre1"], O, t_hb, None, dead)
                        yield
                fg.append(make_hb())
                wd = a["w_dkv"]

                def latent(src, c0, xs, xt, gname, dst, cqd):
                    outs = proj(src, c0, xs, xt, RAWL, r=r_b)
                    for n_, t in enumerate(outs):
                        sq_add(RAWL[:, 2 * n_:2 * n_ + 2, :], t)

                    def norm():
                        d = {}
                        yield from later(2, rstd(512, 1e-6, RS, d))
                        for k_, v in norm_to(RAWL, gcol[gname], dst, 4, d[0]).items():
                            cqd[k_] = v
                    return norm()

                def rope(x, dst, t, res):
                    yield
                    PE.wait(bank_free[7], t)
                    e_ = mm(ps[:, 7, 0:S], C["perm"][:, :], x, True, inc=True)
                    yield
                    i, tm = tmp()
                    t = tt(tm[:, 1, :], ps[:, 7, 0:S], C["sin"][:, :], ALU.mult, e_, tmp_free[i])
                    bank_free[7] = t
                    tc_ = tt(tm[:, 0, :], x, C["cos"][:, :], ALU.mult)
                    t = tt(dst, tm[:, 0, :], tm[:, 1, :], ALU.add, t, tc_)
                    tmp_free[i] = t
                    res[0] = t

                t_ckv, t_cq = {}, {}
                bg.append(latent(wd, 0, H, lambda n: t_kv[n], "ckv", CKV, t_ckv))

                def view(j, k):
                    src = wd[k * P:(k + 1) * P, 512:576]
                    return [(j * P, 64, src), (j * P + 64, 64, src)]
                [(b, t)] = dense(None, 0, 1, list(range(KD)), H, lambda n: t_kv[n], per=8, view=view)
                hkv_dead = (s_pe, PE.n)
                t = sum_pair(KR[:, :].unsqueeze(1), b, t, n=1)
                t = tt(KR[:, :], KR[:, :], RSX[:, :], ALU.mult, t)
                bg.append(rope(KR[:, :], KR[:, :], t, kr))
                need(t_ckv, 3)
                bg.append(latent(a["w_in_b"][0], 0, O, lambda n: need(t_hb, n), "cq", CQ, t_cq))
                w_uq = a["w_uq"][0].rearrange("r (h e) -> r h e", e=192)
                o_tok.clear()
                OB[0], o_war[0] = H, hkv_dead
                for j in range(4):
                    s = j % 2
                    if j >= 2:
                        need(o_tok, 4 * (j - 2) + 3)
                    fr = [slot_pe[s]]
                    tk = proj(a["w_uk"], 512 * j, CKV, lambda n: t_ckv[n], kT[s], nk=4, free=fr)
                    tv = proj(a["w_uv"], 512 * j, CKV, lambda n: t_ckv[n], Vn[s][:, :, :], nk=4, natural=True,
                              free=fr)
                    if s == 1 and j == 1:
                        need(t_cq, 3)
                        fr.append(t_cq[3])

                    def group_g():
                        return proj(a["w_in_b"][0], 512 + 512 * j, O, lambda n: need(t_hb, n), gT[s],
                                    free=fr, r=r_b, silu=True)
                    if j == 0:
                        tg = group_g()
                    vq = lambda jj, k, j=j: [(jj * 512, 512, w_uq[k * P:(k + 1) * P, 4 * j:4 * j + 4, 0:128])]
                    tq = proj(None, 0, CQ, lambda n: need(t_cq, n), qT[s], nk=4, free=fr, view=vq)
                    vr = lambda jj, k, j=j: [(jj * 256, 256, w_uq[k * P:(k + 1) * P, 4 * j:4 * j + 4, 128:192])]
                    tr_ = proj(None, 0, CQ, lambda n: t_cq[n], qR[s], nk=4, free=fr, view=vr, wk=4, nt=2)
                    if j > 0:
                        tg = group_g()
                    qr = [{}, {}]

                    for i in range(2):
                        bg.append(rope(qR[s][:, i, :], qR[s][:, i, :], tr_, qr[i]))
                    for i0 in (0, 2):
                        def both(i0=i0, s=s, j=j, toks=[tk, tq, tr_, tv, tg], qq=qr):
                            yield from attn_b(s, 4 * j + i0, i0, toks, [kr[0], qq[0][0], qq[1][0]])
                        bg.append(both())
                cq_dead = (s_pe, PE.n)
                late.pop("p")

                def p_again():
                    late["p"] = p_split(t_p1, cq_dead)
                    yield
                bg.append(p_again())
                t_h2, dead = mixer_tail(1, a["w_out_b"][0], a["w_ple_proj"][1], a["w_ple_gate"][1],
                                        lambda c, toks, t, w_: gained(c, gcol["mixpre"], H, toks, t, w_))
            if stop not in ("a", "b"):
                r_c = {}
                bg.append(later(2, rstd(D, 1e-6, RSX, r_c, True)))
                i = small[0]
                small[0] += 1
                GP.wait(late["bv"], late["p"][1], dead)
                for h in range(8):
                    src = bass.AP(bvd.tensor, h * 384, [[1, P], [1, S]])
                    rt_tok = GP.dma(lambda e, h=h, src=src: e.dma_start(RT[:, h, :], src), s_in[i], 16 * (h + 1))
                th2 = lambda n: t_h2[n]
                w = a["w_in_2"][0]
                o_tok.clear()
                OB[0], o_war[0] = O, dead
                for j in range(2):
                    fr = [slot_pe[j], st["xr"]]
                    tq = proj(w, 512 * j, H, th2, qT[j], scale=0.125, free=fr, r=r_c)
                    tk = proj(w, 1024 + 512 * j, H, th2, kT[j], free=fr, r=r_c)
                    tv = proj(w, 2048 + 512 * j, H, th2, Vn[j][:, :, :], natural=True, free=fr, r=r_c)
                    for i in range(4):
                        bg.append(attn_c(j, 4 * j + i, i, [tq, tk, tv], rt_tok))
                for m in range(2):
                    tg_ = proj(w, 4096 + 512 * m, H, th2, GC, r=r_c)
                    outs = summed(dense(w, 5120 + 512 * m, 4, list(range(KD)), H, th2), r_c)
                    t_u = []
                    for n_, (i, tm, t) in enumerate(outs):
                        g = GC[:, 2 * n_:2 * n_ + 2, :]
                        tmp_free[i] = t = tt(g, g, tm, ALU.mult, t, tg_)
                        t_u.append(t)
                    toks = dense(w, 3072 + 512 * m, 4, list(range(KD)), H, th2)
                    if m == 1:
                        need(o_tok, 3)
                        DV.wait(slot_pe[0])
                    for n_ in range(2):
                        for jj in range(2):
                            ch = 4 * m + 2 * n_ + jj
                            u, y = GC[:, 2 * n_ + jj, :], CT[m][:, 2 * n_ + jj, :]
                            cw = [GAIN[:, gcol[f"cw{q}"] + ch:gcol[f"cw{q}"] + ch + 1] for q in range(3)]
                            t = ts(y, u, cw[2], None, ALU.mult, None, t_u[n_])
                            t = stt(y[:, 1:S], u[:, 0:S - 1], cw[1], y[:, 1:S], ALU.mult, ALU.add, t)
                            t_y = stt(y[:, 2:S], u[:, 0:S - 2], cw[0], y[:, 2:S], ALU.mult, ALU.add, t)
                    for n_, (i, tm, t) in enumerate(summed(toks, r_c)):
                        c2 = CT[m][:, 2 * n_:2 * n_ + 2, :]
                        tmp_free[i] = t = tt(c2, c2, tm, ALU.mult, t, t_y)
                        sq_add(c2, t)
                h2_dead = (s_pe, PE.n)

                def conv_norm():
                    d = {}
                    yield from later(2, rstd(1024, 1e-6, RS, d))
                    cn = gcol["cn"]
                    for c in range(0, 8, 2):
                        i, tm = tmp()
                        for j in range(2):
                            t = stt(tm[:, j, :], CT[c // 4][:, c % 4 + j, :], GAIN[:, cn + c + j:cn + c + j + 1], RS[:, :],
                                    ALU.mult, ALU.mult, d[0], tmp_free[i])
                        t = split_x(tm[:, :, :], O, 8 + c, 2, t)
                        tmp_free[i] = t
                        o_tok[8 + c] = o_tok[9 + c] = t
                        yield
                bg.append(conv_norm())
                out_proj(a["w_out_2"][0], list(range(KD)), O, lambda n: need(o_tok, n), T)
                r = rstd_now(D, 1e-6)
                t_h3, r_d = {}, {}

                def h3(c, t):
                    gained(c, gcol["ffnpre"], H, t_h3, t, h2_dead)
                    st["xr"] = sq_add(xT[:, c:c + 2, :], t)
                    if c == KD - 2:
                        bg.append(later(1, rstd(D, 1e-6, RSX, r_d)))
                at_once(fg, residual(T, gcol["mixpost"], r, None, h3), 1)
            if stop not in ("a", "b", "c"):
                th3 = lambda n: need(t_h3, n)
                wg, wu, wdn = a["w_gate_2"][0], a["w_up_2"][0], a["w_down_2"][0]
                acts_free = (s_pe, PE.n)
                for part, (f0, f1) in enumerate(((0, 6), (6, 11))):
                    a_tok = {}
                    for f in range(f0, f1):
                        toks = dense(wg, 512 * f, 4, list(range(KD)), H, th3)
                        need(t_h3, KD - 1)
                        sg = finish(toks, SG, r=r_d, silu=True)
                        toks = dense(wu, 512 * f, 4, list(range(KD)), H, th3)
                        for n_, (i, tm, t) in enumerate(summed(toks, r_d)):
                            t = tt(tm, tm, SG[:, 2 * n_:2 * n_ + 2, :], ALU.mult, t, sg[n_])
                            k = 4 * (f - f0) + 2 * n_
                            t = split_x(tm, ACTS, k, 2, t, acts_free)
                            tmp_free[i] = t
                            a_tok[k] = a_tok[k + 1] = t
                    out_proj(wdn, list(range(4 * f0, 4 * f1)), ACTS, lambda n: a_tok[n], T2,
                             first=(part == 0), last=(part == 1))
                    acts_free = (s_pe, PE.n)
                r = rstd_now(D, 1e-6)
                last_pe = (s_pe, PE.n)
                x_done = {}

                def note(c, t):
                    x_done[c] = t
                fin = residual(T2, gcol["ffnpost"], r, None, note)
            else:
                for q in (fg, bg):
                    while q:
                        step(q)
                last_pe = (s_pe, PE.n)
                x_done = {c: (s_dve, DV.n) for c in range(0, KD, 2)}
                fin = iter(range(8))
            y = out.rearrange("a (t p) d -> p (a t) d", p=P)
            nout = 0
            for m in range(4):
                next(fin)
                next(fin)
                for t in range(2):
                    b = take(2)
                    PE.wait(bank_free[b], x_done[4 * m + 2])
                    for j in range(4):
                        e_ = tr(ps[:, b, j * P:(j + 1) * P], xT[:, 4 * m + j, t * P:(t + 1) * P], inc=(j == 3))
                    d = YN[:, t, 512 * m:512 * m + 512]
                    t_ = act(d, ps[:, b, :], ACT.Copy, e_, last_pe)
                    bank_free[b] = t_
                    nout += 16
                    SP.dma(lambda e, d=d, t=t, m=m: e.dma_start(y[:, t, 512 * m:512 * m + 512], d), s_out,
                           nout, t_)
            SP.wait(late["bv"], (s_out, nout))
            return chunks, PE, AC, DV, SP, GP

        chunks, *_ = program([])
        _, PE, AC, DV, SP, GP = program(chunks)
        s_n = sem("s_n")
        block = ctx.enter_context(nc.Block())

        @block.tensor
        def _(e):
            e.wait_ge(s_n, 1)
            PE.play(e)

        @block.vector
        def _(e):
            e.memset(NONES[:, :], -1.0).then_inc(s_n, 1)
            DV.play(e)

        @block.scalar
        def _(e):
            AC.play(e)

        @block.gpsimd
        def _(e):
            GP.play(e)

        @block.sync
        def _(e):
            SP.play(e)


_INS = ["x", "p", "norm_pre", "norm_post", "w_in_a", "w_out_a", "w_in_b", "q_latent_norm", "w_uq", "w_out_b",
        "kv_norm", "w_dkv", "kv_latent_norm", "w_uk", "w_uv", "w_ple_proj", "w_ple_gate", "w_in_2", "w_out_2",
        "lambda_q1_2", "lambda_k1_2", "lambda_q2_2", "lambda_k2_2", "subln_gain_2", "conv_w_2",
        "conv_norm_gain_2", "rel_bias_2", "w_gate_2", "w_up_2", "w_down_2", "norm_mix_pre_2",
        "norm_mix_post_2", "norm_ffn_pre_2", "norm_ffn_post_2"]


def constants():
    f = np.float32
    i = np.arange(P)
    t = {}
    t["ident"] = np.eye(P, dtype=f)
    t["flip"] = np.eye(P, dtype=f)[::-1]
    t["tri"] = -(i[:, None] >= i[None, :]).astype(f)
    t["ones"] = np.ones((P, P), f)
    perm = np.zeros((P, P), f)
    perm[i ^ 32, i] = 1.0
    t["perm"] = perm
    t["mask"] = (i[:, None] < i[None, :]).astype(f)
    t["negA"] = np.where(i[:, None] >= i[None, :], f(-1e30), f(0))
    t["negB"] = np.where((i[:, None] < 64) & (i[None, :] >= 64), f(-1e30), f(0))
    inv = (f(1.0) / (f(10000.0) ** (np.arange(0, 64, 2, dtype=f) / f(64)))).astype(f)
    ang = np.arange(S, dtype=f)[None, :] * inv[i % 32][:, None]
    t["cos"] = np.cos(ang).astype(f)
    t["sin"] = (np.sin(ang) * np.where(i % 64 < 32, -1.0, 1.0)[:, None]).astype(f)
    cst = np.concatenate([t[n].astype(f) for n in CONST], axis=1)
    d = 255 - np.arange(384)
    n = np.maximum(d, 0)
    nf = np.maximum(n, 16).astype(f)
    large = 16 + (np.log(nf / f(16)) / f(math.log(8.0)) * f(16)).astype(np.int32)
    large = np.minimum(large, 31)
    bucket = np.where(n < 16, n, large)
    oh = np.zeros((33, 384), f)
    oh[bucket, np.arange(384)] = 1.0
    oh[32] = np.where(d < 0, f(-1e30), f(0))
    return np.ascontiguousarray(cst), oh


def kernel(**inputs):
    import concourse.bacc as _bacc
    from concourse.bass_utils import run_bass_kernel_spmd as _run

    nc = _bacc.Bacc("TRN2", target_bir_lowering=False, num_devices=1)
    arrays, aps = {}, {}
    for name in _INS:
        v = np.ascontiguousarray(inputs[name])
        arrays[f"in_{name}"] = v
        aps[name] = nc.dram_tensor(f"in_{name}", v.shape, mybir.dt.from_np(v.dtype), kind="ExternalInput").ap()
    cst, oh = constants()
    arrays["cst"], arrays["oh"] = cst, oh
    c_ap = nc.dram_tensor("cst", cst.shape, F32, kind="ExternalInput").ap()
    o_ap = nc.dram_tensor("oh", oh.shape, F32, kind="ExternalInput").ap()
    y = nc.dram_tensor("out", (1, S, D), F32, kind="ExternalOutput").ap()
    build(nc, aps, c_ap, o_ap, y, STOP)
    r = _run(nc, [arrays], core_ids=[0])
    return r.results[0]["out"]


STOP = None
```

```python
import math
from contextlib import ExitStack

import numpy as np
import concourse.bass as bass
from concourse import mybir

F32 = mybir.dt.float32
F32R = mybir.dt.float32r
BF16 = mybir.dt.bfloat16
ALU = mybir.AluOpType
ACT = mybir.ActivationFunctionType
AX = mybir.AxisListType

P = 128
S = 256
D = 2048
KD = D // P
ROWS = [("pre0", 16), ("pre1", 16), ("mixpre", 16), ("post0", 16), ("post1", 16), ("kv", 16), ("mixpost", 16),
        ("ffnpre", 16), ("ffnpost", 16), ("ckv", 4), ("cq", 4), ("cw0", 8), ("cw1", 8), ("cw2", 8), ("cn", 8),
        ("sub", 1)]
DFF = 5632
NRAW = 3
NSPL = 4
AHEAD = 4
CH = 1024
CONST = ["ident", "flip", "tri", "ones", "perm", "mask", "cos", "sin", "negones"]
CW = {"cos": 256, "sin": 256}


class Queue:

    def __init__(self, sem):
        self.sem, self.n, self.ops, self.seen = sem, 0, [], {}

    def wait(self, *tokens):
        for t in tokens:
            if t is None:
                continue
            if isinstance(t, list):
                self.wait(*t)
                continue
            sem, value = t
            if self.seen.get(sem, 0) < value:
                self.seen[sem] = value
                self.ops.append(lambda e, sem=sem, value=value: e.wait_ge(sem, value))

    def do(self, fn, *tokens, inc=True):
        self.wait(*tokens)
        if not inc:
            self.ops.append(fn)
            return None
        self.n += 1
        self.ops.append(lambda e: fn(e).then_inc(self.sem, 1))
        return (self.sem, self.n)

    def dma(self, fn, sem, value, *tokens):
        self.wait(*tokens)
        self.ops.append(lambda e: fn(e).then_inc(sem, 16))
        return (sem, value)

    def play(self, eng):
        for op in self.ops:
            op(eng)


def build(nc, a, cst, onehot, gains, lams, out):
    ctx = ExitStack()
    with ctx:
        BASE = 16512
        pos = [BASE]

        def at(name, shape, dt, off):
            return nc.alloc_sbuf_tensor_at(name, shape, dt, offset=off)

        def sb(name, shape, dt=F32):
            n = int(np.prod(shape[1:])) * (2 if dt == BF16 else 4)
            t = at(name, shape, dt, pos[0])
            pos[0] += (n + 31) // 32 * 32
            return t

        xT = sb("xT", [P, KD, S])
        H = sb("H", [P, KD, 2 * S], F32R)
        R1 = pos[0]
        O = at("O", [P, KD, 2 * S], F32R, R1)
        SL = [R1 + 32768 + 18432 * s for s in range(2)]
        qT = [at(f"qT{s}", [P, 4, S], F32, SL[s]) for s in range(2)]
        kT = [at(f"kT{s}", [P, 4, S], F32, SL[s] + 4096) for s in range(2)]
        Vn = [at(f"Vn{s}", [P, 2, 512], F32, SL[s] + 8192) for s in range(2)]
        gT = [at(f"gT{s}", [P, 4, S], F32, SL[s] + 12288) for s in range(2)]
        qR = [at(f"qR{s}", [P, 2, S], F32, SL[s] + 16384) for s in range(2)]
        T = at("T", [P, KD, S], F32, SL[0])
        PP = at("PP", [P, KD, S], F32, SL[1])
        RAWL = [at(f"RAWL{i}", [P, 4, S], F32, SL[1 - i]) for i in range(2)]
        GC = at("GC", [P, 4, S], F32, SL[0] + 12288)
        CT = [at(f"CT{m}", [P, 4, S], F32, SL[1 - m] + 12288 * (1 - m)) for m in range(2)]
        XNAT = at("XNAT", [P, 2, D], F32, BASE + 16384)
        TNAT = at("TNAT", [P, 2, D], F32, BASE + 32768)
        ACTS = at("ACTS", [P, 24, 2 * S], F32R, R1)
        T2 = at("T2", [P, KD, S], F32, R1 + 49152)
        SG = at("SG", [P, 4, S], F32, R1 + 65536)
        XN = at("XN", [P, 2, D], F32, SL[0])
        GN = at("GN", [P, 2, P], F32, SL[1])
        OH = at("OH", [32, 384], F32, SL[1] + 1024)
        RB = at("RB", [32, 8], F32, SL[1] + 2560)
        MR = at("MR", [1, 384], F32, SL[1] + 2592)
        BV = at("BV", [8, 384], F32, SL[1] + 4128)
        LM = at("LM", [1, 4, 64], F32, SL[1] + 5664)
        LP = at("LP", [1, 2, 64], F32, SL[1] + 6688)
        LS = at("LS", [1, 8], F32, SL[1] + 7200)
        NG = at("NG", [P, 2, P], F32, SL[1] + 7232)
        pos[0] = R1 + 69632
        L1 = pos[0]
        CKV = sb("CKV", [P, 4, 2 * S], F32R)
        CQ = sb("CQ", [P, 4, 2 * S], F32R)
        RT = at("RT", [P, 8, S], F32, L1)
        KR = sb("KR", [P, S])
        PN = sb("PN", [P, 2, S])
        RAW = sb("RAW", [P, NRAW, CH])
        WH = sb("WH", [P, NSPL, CH], F32R)
        WL = sb("WL", [P, NSPL, CH], F32R)
        NCST = sum(CW.get(n, P) for n in CONST)
        CS = sb("CS", [P, NCST])
        C, off = {}, 0
        for n in CONST:
            C[n] = CS[:, off:off + CW.get(n, P)]
            off += CW.get(n, P)
        identb = sb("identb", [P, P], BF16)
        negb = [sb(f"negb{i}", [P, P], BF16) for i in range(2)]
        GAIN = sb("GAIN", [P, 256])
        NLAM = sb("NLAM", [P, 3])
        TMP = [sb(f"TMP{i}", [P, 2, S]) for i in range(2)]
        SQ = sb("SQ", [P, 2, S])
        ACC = sb("ACC", [P, 2, S])
        RSX = sb("RSX", [P, S])
        RS = sb("RS", [P, S])
        RC = sb("RC", [P, 2])
        F1 = sb("F1", [P, 2, 384])
        F2 = sb("F2", [P, 2, 384])
        RV, RW = SQ[:, 0, :], SQ[:, 1, :]
        SM = sb("SM", [P, 16])
        TMPG = [sb(f"TMPG{i}", [P, 2, S]) for i in range(2)]
        if pos[0] > 229344:
            raise ValueError(f"SBUF over by {pos[0] - 229344}")

        ps = ctx.enter_context(nc.psum_tensor("ps", [P, 8, 512], F32))
        bvd = nc.dram_tensor("bvd", (8, 384), F32, kind="Internal").ap()

        def sem(name):
            return ctx.enter_context(nc.semaphore(name))

        s_pe, s_act, s_dve = sem("s_pe"), sem("s_act"), sem("s_dve")
        s_raw = [sem(f"s_raw{i}") for i in range(NRAW)]
        s_in = [sem(f"s_in{i}") for i in range(20)]
        s_out = sem("s_out")

        def program(chunks_known):
            PE, AC, DV, SP, GP = Queue(s_pe), Queue(s_act), Queue(s_dve), Queue(None), Queue(None)
            chunks = []

            def V(fn, *t):
                return DV.do(fn, *t)

            def A(fn, *t):
                return AC.do(fn, *t)

            table = [None]

            def act(o, i, f, *t, **kw):
                need = 1 if f in (ACT.Exp, ACT.Ln) else 2 if f in (ACT.Silu, ACT.Sigmoid) else table[0]
                if need == 1 and table[0] != 1:
                    AC.do(lambda e: e.preload_act_table_set("natural_log_exp_and_others"), inc=False)
                table[0] = need
                return A(lambda e: e.activation(o, i, f, **kw), *t)

            def tt(o, x, y, op, *t):
                return V(lambda e: e.tensor_tensor(o, x, y, op), *t)

            def ts(o, x, s1, s2, op0, op1, *t):
                if op1 is None:
                    return V(lambda e: e.tensor_scalar(o, x, s1, None, op0), *t)
                return V(lambda e: e.tensor_scalar(o, x, s1, s2, op0, op1), *t)

            def stt(o, x, s, y, op0, op1, *t):
                return V(lambda e: e.scalar_tensor_tensor(out=o, in0=x, scalar=s, in1=y, op0=op0, op1=op1), *t)

            def mm(o, l, r, start=False, *t, inc=False):
                return PE.do(lambda e: e.matmul(o, l, r, start=start, stop=True, skip_group_check=True), *t, inc=inc)

            def tr(o, i, *t, inc=False):
                idn = C["ident"] if i.shape[0] == P else C["ident"][0:i.shape[0], 0:i.shape[0]]
                return PE.do(lambda e: e.transpose(o, i, idn), *t, inc=inc)

            small = [0]

            def load(dst, src, q=None, *t):
                i = small[0]
                small[0] += 1
                return (q or GP).dma(lambda e: e.dma_start(dst, src), s_in[i], 16, *t)

            raw_count = [0] * NRAW
            raw_tok, raw_free = {}, {}
            spl_tok, spl_free = {}, {}
            loaded, split = [0], [0]

            def load_chunk():
                i = loaded[0]
                if i >= len(chunks_known):
                    return
                loaded[0] += 1
                slot = i % NRAW
                SP.wait(raw_free.get(i - NRAW))
                for off, n, src in chunks_known[i][0]:
                    dst = RAW[:, slot, off:off + n] if n else RAW[:, slot, :].rearrange(
                        "p (a b) -> p a b", b=P)[:, :, off:off + 64]
                    raw_count[slot] += 16
                    if n and len(src.shape) == 3:
                        dst = dst.rearrange("p (a b) -> p a b", a=src.shape[1])
                    raw_tok[i] = SP.dma(lambda e, dst=dst, src=src: e.dma_start(dst, src),
                                        s_raw[slot], raw_count[slot])

            def split_chunk():
                i = split[0]
                if i >= len(chunks_known):
                    return
                split[0] += 1
                r, w, n = i % NRAW, i % NSPL, chunks_known[i][1]
                raw, hi, lo = RAW[:, r, 0:n], WH[:, w, 0:n], WL[:, w, 0:n]
                th = act(hi, raw, ACT.Copy, raw_tok[i], spl_free.get(i - NSPL))
                spl_tok[i] = tt(lo, raw, hi.bitcast(F32), ALU.subtract, th)
                raw_free[i] = [th, spl_tok[i]]
                load_chunk()

            def split_early():
                if chunks_known and split[0] < len(chunks_known) and split[0] - NSPL in spl_free:
                    split_chunk()

            def next_chunk(parts, n):
                i = len(chunks)
                chunks.append((parts, n))
                if chunks_known:
                    while split[0] <= min(i + AHEAD - 1, len(chunks_known) - 1):
                        split_chunk()
                return i

            bg = []

            fg = []

            def step(q):
                while q:
                    try:
                        next(q[0])
                        return
                    except StopIteration:
                        q.pop(0)

            def drain():
                while bg:
                    step(bg)

            def at_once(q, gen, n=0):
                for _ in range(n):
                    next(gen)
                q.append(gen)

            def need(d, n):
                while n not in d:
                    step(fg)
                    if n not in d:
                        step(bg)
                return d[n]

            bank_free = {b: None for b in range(8)}
            ring = [0]

            def take(n):
                b = ring[0]
                ring[0] = (b + n) % 6
                return b

            def dense(src, c0, nt, kts, xs, xt, per=2, natural=False, view=None, banks=None):
                nk = len(kts)
                if banks is None:
                    b0 = take(2 if natural else (nt + 1) // 2 * 2)
                    banks = [(b0 + t) % 6 for t in range(nt)]
                w = nt * P
                toks = []
                for ci in range(0, nk, per):
                    ks = kts[ci:ci + per]
                    if view:
                        parts = [p for j, k in enumerate(ks) for p in view(j, k)]
                    else:
                        parts = [(0, len(ks) * w, src[ks[0] * P:(ks[-1] + 1) * P, c0:c0 + w]
                                  .rearrange("(c p) n -> p c n", p=P))]
                    i = next_chunk(parts, len(ks) * w)
                    if chunks_known:
                        PE.wait(spl_tok[i])
                    hi = WH[:, i % NSPL, 0:len(ks) * w].rearrange("p (c n) -> p c n", n=w)
                    lo = WL[:, i % NSPL, 0:len(ks) * w].rearrange("p (c n) -> p c n", n=w)
                    last_chunk = ci + per >= nk
                    if natural:
                        if ci == 0:
                            PE.wait(bank_free[b0], bank_free[b0 + 1])
                        for j, k in enumerate(ks):
                            n = ci + j
                            PE.wait(xt(n))
                            for t in range(2):
                                xh = xs[:, n, t * P:(t + 1) * P]
                                xl = xs[:, n, S + t * P:S + (t + 1) * P]
                                o = ps[:, b0 + t, :]
                                mm(o, xh, hi[:, j, :], n == 0)
                                mm(o, xh, lo[:, j, :])
                                end = mm(o, xl, hi[:, j, :], inc=(t == 1 and j == len(ks) - 1))
                        if last_chunk:
                            toks.append((b0, end))
                    else:
                        for t in range(nt):
                            b = banks[t]
                            if ci == 0:
                                PE.wait(bank_free[b])
                            for j, k in enumerate(ks):
                                n = ci + j
                                PE.wait(xt(n))
                                wh, wl = hi[:, j, t * P:(t + 1) * P], lo[:, j, t * P:(t + 1) * P]
                                mm(ps[:, b, :], wh, xs[:, n, :], n == 0)
                                fin = j == len(ks) - 1 and (t == nt - 1 or (last_chunk and t % 2 == 1))
                                end = mm(ps[:, b, S:2 * S], wl, xs[:, n, 0:S], inc=fin)
                            if last_chunk and (t % 2 == 1 or t == nt - 1):
                                toks.append((b - t % 2, end))
                    spl_free[i] = end
                    step(fg)
                    step(bg)
                return toks

            def halves(b, n=2):
                return ps[:, b:b + n, 0:S], ps[:, b:b + n, S:2 * S]

            def release(b, tok, n=2):
                for i in range(n):
                    bank_free[b + i] = tok

            def sum_pair(o, b, tok, *t, n=2):
                x, y = halves(b, n)
                r = act(o, y, ACT.Copy, tok, *t)
                r = tt(o, x, o, ALU.add, r)
                release(b, r, n)
                return r

            tmp_free = [None, None]
            tmp_at = [0]

            def tmp():
                i = tmp_at[0]
                tmp_at[0] = 1 - i
                return i, TMP[i]

            def bc(ap, n=2):
                return ap.unsqueeze(1).broadcast_to([P, n, ap.shape[-1]])

            def split_x(src, dst, k0, n, dep, *war):
                th = act(dst[:, k0:k0 + n, 0:S], src, ACT.Copy, dep, *war)
                return tt(dst[:, k0:k0 + n, S:2 * S], src, dst[:, k0:k0 + n, 0:S].bitcast(F32),
                          ALU.subtract, th)

            st = {"first": True, "acc": None, "accfree": None}
            sq_free, sq_open = [None], []

            def sq_pe(src, dep, i):
                buf = (ACC, SQ)[i % 2]
                t = act(buf[:, :, :], src, ACT.Square, dep, sq_free[0] if i % 2 else st["accfree"])

                def add():
                    PE.wait(t, bank_free[6] if i == 0 else None)
                    mm(ps[:, 6, 0:S], C["ones"], buf[:, 0, :], i == 0)
                    t2 = mm(ps[:, 6, 0:S], C["ones"], buf[:, 1, :], inc=True)
                    st["bank"] = t2
                    if i % 2:
                        sq_free[0] = t2
                    else:
                        st["accfree"] = t2
                return add

            def sq_add(src, dep, defer=False):
                if st["first"]:
                    st["acc"] = act(ACC[:, :, :], src, ACT.Square, dep, st["accfree"])
                    st["first"] = False
                    return st["acc"]
                flush()
                t = act(SQ[:, :, :], src, ACT.Square, dep, sq_free[0])

                def add():
                    st["acc"] = sq_free[0] = tt(ACC[:, :, :], ACC[:, :, :], SQ[:, :, :], ALU.add, t, st["acc"])
                sq_open.append(add)
                if not defer:
                    flush()
                return t

            def flush():
                if sq_open:
                    sq_open.pop()()

            chains = [0]

            def later(n, gen):
                while chains[0]:
                    yield
                for _ in range(n):
                    yield
                yield from gen

            def rstd(dim, eps, rs, done, cols=False, ring_bank=False):
                b, t = 6, st.pop("bank", None)
                if t is None:
                    b = take(2) if ring_bank else 6
                    flush()
                    PE.wait(bank_free[b], st["acc"])
                    mm(ps[:, b, 0:S], C["ones"], ACC[:, 0, :], True)
                    t = mm(ps[:, b, 0:S], C["ones"], ACC[:, 1, :], inc=True)
                    st["accfree"], st["first"] = t, True
                t = ts(RV, ps[:, b, 0:S], 1.0 / dim, eps, ALU.mult, ALU.add, t)
                bank_free[b] = t
                sq_free[0] = t = rsqrt(rs[:, :], RV, RW, t)
                if cols:
                    yield
                    yield
                    yield
                    PE.wait(bank_free[7], t)
                    tr(ps[:, 7, 0:P], rs[:, 0:P])
                    t2 = tr(ps[:, 7, P:S], rs[:, P:S], inc=True)
                    t2 = V(lambda e: e.tensor_copy(RC[:, :], ps[:, 7, 0:S:P]), t2)
                    bank_free[7] = t2
                    t = [t, t2]
                done[0] = t

            def rstd_now(dim, eps, rs=None):
                drain()
                d = {}
                for _ in rstd(dim, eps, rs or RS, d):
                    pass
                return d[0]

            def rsqrt(o, v, w, dep):
                split_early()
                t = act(w, v, ACT.Ln, dep)
                t = act(o, w, ACT.Exp, t, scale=-0.5)
                t = stt(w, o, -0.5, o, ALU.mult, ALU.mult, t)
                t = tt(w, w, v, ALU.mult, t)
                return stt(o, w, 1.5, o, ALU.add, ALU.mult, t)

            def norm_to(src, g0, dst, n, r, toks):
                for c in range(0, n, 2):
                    i, tm = tmp()
                    for j in range(2):
                        t = stt(tm[:, j, :], src[:, c + j, :], GAIN[:, g0 + c + j:g0 + c + j + 1], RS[:, :],
                                ALU.mult, ALU.mult, r, tmp_free[i])
                    t = split_x(tm[:, :, :], dst, c, 2, t)
                    tmp_free[i] = t
                    toks[c] = toks[c + 1] = t
                    yield

            def gained(c, g0, dst, toks, dep, *war, defer=False):
                gs = [GAIN[:, g0 + c + j:g0 + c + j + 1] for j in range(2)]
                for j in range(2):
                    th = act(dst[:, c + j, 0:S], xT[:, c + j, :], ACT.Copy, dep, *war, scale=gs[j])

                def low():
                    for j in range(2):
                        t = stt(dst[:, c + j, S:2 * S], xT[:, c + j, :], gs[j], dst[:, c + j, 0:S].bitcast(F32),
                                ALU.mult, ALU.subtract, th)
                    toks[c] = toks[c + 1] = t
                if defer:
                    return low
                low()

            t_ident = load(CS[:, 0:P], cst[:, 0:P], SP)
            xr = a["x"].rearrange("a (t p) d -> p (a t) d", p=P)
            t_x = []
            for m in range(4):
                t_x.append(load(XN[:, :, 512 * m:512 * m + 512], xr[:, :, 512 * m:512 * m + 512], SP))
                if chunks_known and m < NRAW:
                    load_chunk()
            gcol = {n: sum(r for _, r in ROWS[:i]) for i, (n, r) in enumerate(ROWS)}
            nrow2 = sum(r for _, r in ROWS) - P
            t_g0 = load(GN[:, 0, :], gains[0:P, :], AC)
            t_cst = load(CS[:, P:NCST], cst[:, P:NCST], AC)
            t_neg = load(NG[:, :, :], cst[:, NCST:NCST + 2 * P].rearrange("p (a b) -> p a b", a=2), AC)
            t_p = load(PN[:, :, :], a["p"][0, 0].rearrange("(t p) d -> p t d", p=P))
            t_g = load(GN[0:nrow2, 1, :], gains[P:P + nrow2, :])
            t_oh = load(OH[:, :], onehot[0:32, :])
            t_mr = load(MR[:, :], onehot[32:33, :])
            t_rb = load(RB[:, :], a["rel_bias_2"])
            t_lm = load(LM[:, :, :], lams)

            PE.wait(t_ident, t_g0)
            t = tr(ps[:, 7, 0:P], GN[:, 0, :], inc=True)
            t_g0 = V(lambda e: e.tensor_copy(GAIN[:, 0:P], ps[:, 7, 0:P]), t)
            bank_free[7] = t_g0
            t_h = {}

            def fetch(c):
                b = 4 + c // 2 % 2
                PE.wait(bank_free[b])
                for j in range(2):
                    for t in range(2):
                        e_ = tr(ps[:, b, j * S + t * P:j * S + (t + 1) * P],
                                XN[:, t, (c + j) * P:(c + j + 1) * P], t_x[c // 4], inc=(j == 1 and t == 1))
                t_v = V(lambda e: e.tensor_copy(
                    xT[:, c:c + 2, :], ps[:, b, :].rearrange("p (j s) -> p j s", j=2)), e_)
                bank_free[b] = t_v
                return t_v

            def x_in():
                t_n = fetch(0)
                for c in range(0, KD, 2):
                    t_v = t_n
                    if c + 2 < KD:
                        t_n = fetch(c + 2)
                    gained(c, gcol["pre0"], H, t_h, [t_v, t_g0])
                    yield
                for c in range(0, KD, 2):
                    sq_add(xT[:, c:c + 2, :], t_n, defer=True)
                    yield
                flush()
                t_h["sq"] = True

            at_once(fg, x_in(), 2)
            r_a, late = {}, {}

            def p_split(t_p, *war):
                PE.wait(bank_free[7], t_p, *war)
                for k in range(2):
                    for t in range(2):
                        e_ = tr(ps[:, 7, k * S + t * P:k * S + (t + 1) * P], PN[:, t, k * P:(k + 1) * P],
                                inc=(k == 1 and t == 1))
                i, tm = tmp()
                t = V(lambda e: e.tensor_copy(tm[:, :, :], ps[:, 7, :].rearrange("p (k s) -> p k s", k=2)),
                      e_, tmp_free[i])
                bank_free[7] = t
                t = split_x(tm[:, :, :], CQ, 0, 2, t, *war)
                tmp_free[i] = t
                return [e_, t]

            def setup_late():
                yield from rstd_first()
                PE.wait(bank_free[7], t_g)
                t = tr(ps[:, 7, 0:nrow2], GN[0:nrow2, 1, :], inc=True)
                t = V(lambda e: e.tensor_copy(GAIN[:, P:P + nrow2], ps[:, 7, 0:nrow2]), t)
                bank_free[7] = t
                s0 = gcol["sub"]
                ts(GAIN[:, s0:s0 + 1], GAIN[:, s0:s0 + 1], 0.8, None, ALU.mult, None, t)
                yield
                V(lambda e: e.tensor_copy(identb[:, :], C["ident"]), t_cst)
                for j in range(2):
                    V(lambda e, j=j: e.tensor_copy(negb[j][:, :], NG[:, j, :]), t_neg)
                yield
                PE.wait(bank_free[6], t_oh, t_rb, t_mr)
                mm(ps[0:8, 6, 0:384], RB[:, :], OH[:, :], True)
                t = mm(ps[0:8, 6, 0:384], C["ones"][0:1, 0:8], MR[:, :], inc=True)
                t = V(lambda e: e.tensor_copy(BV[:, :], ps[0:8, 6, 0:384]), t)
                bank_free[6] = t
                late["bv"] = load(bvd, BV[:, :], GP, t)
                yield
                t = tt(LP[:, :, :], LM[:, 0:4:2, :], LM[:, 1:4:2, :], ALU.mult, t_lm)
                t = V(lambda e: e.tensor_reduce(LS[:, 0:2], LP[:, :, :], AX.X, ALU.add), t)
                t = act(LS[:, 2:4], LS[:, 0:2], ACT.Exp, t)
                t = tt(LS[:, 4:5], LS[:, 3:4], LS[:, 2:3], ALU.subtract, t)
                t = ts(LS[:, 4:5], LS[:, 4:5], -(0.8 - 0.6 * math.exp(0.0)), None, ALU.add, None, t)
                t = stt(LS[:, 7:8], LS[:, 4:5], -1.0, LS[:, 4:5], ALU.mult, ALU.max, t)
                t = ts(LS[:, 7:8], LS[:, 7:8], 1.0, None, ALU.max, None, t)
                t = V(lambda e: e.reciprocal(LS[:, 5:6], LS[:, 7:8]), t)
                t = tt(LS[:, 4:5], LS[:, 4:5], LS[:, 5:6], ALU.mult, t)
                t = stt(LS[:, 6:7], LS[:, 5:6], 1e-5, LS[:, 5:6], ALU.mult, ALU.mult, t)
                yield
                yield
                PE.wait(bank_free[7], t)
                t = mm(ps[:, 7, 0:3], C["ones"][0:1, :], LS[:, 4:7], True, inc=True)
                t = V(lambda e: e.tensor_copy(NLAM[:, :], ps[:, 7, 0:3]), t)
                bank_free[7] = t
                late["t"] = t
                yield
                late["p"] = p_split(t_p)

            def rstd_first():
                while "sq" not in t_h:
                    yield
                yield
                yield
                PE.wait(t_cst)
                yield from rstd(D, 1e-6, RSX, r_a, True)

            bg.append(setup_late())
            OB, o_war = [O], [None]
            o_tok = {}
            slot_pe = [None, None]

            f_free = {"F1": None, "F2": None}

            def pv(slot, vi, nb, w_tok, v_tok):
                for j in range(nb):
                    PE.wait(w_tok, v_tok)
                    vc = (vi + j) * P
                    mm(ps[:, 6 + j, 0:S], Vn[slot][:, 0, vc:vc + P], F1[:, j, 0:S], True)
                    t = mm(ps[:, 6 + j, P:S], Vn[slot][:, 1, vc:vc + P], F1[:, j, S:384], inc=(j == nb - 1))
                f_free["F1"] = t
                slot_pe[slot] = t
                return t

            def gate_out(slot, gi_, h0, t, g_tok):
                i, tm = tmp()
                t = tt(tm[:, :, :], ps[:, 6:8, 0:S], gT[slot][:, gi_:gi_ + 2, :], ALU.mult, t, g_tok, tmp_free[i])
                release(6, t)
                t = split_x(tm[:, :, :], OB[0], h0, 2, t, o_war[0])
                tmp_free[i] = t
                o_tok[h0] = o_tok[h0 + 1] = t

            def attn_a(slot, h0, i0, toks):
                PE.wait(bank_free[6], bank_free[7], toks[0:2])
                for j in range(2):
                    q, k = qT[slot][:, i0 + j, :], kT[slot][:, i0 + j, :]
                    mm(ps[:, 6 + j, 0:S], k[:, 0:P], q, True)
                    t = mm(ps[:, 6 + j, S:384], k[:, P:S], q[:, P:S], inc=(j == 1))
                yield
                z = ps[:, 6:8, 0:384]
                t = act(F1[:, :, :], z, ACT.Abs, t, f_free["F1"])
                t = act(F1[:, :, :], F1[:, :, :], ACT.Exp, t, scale=-1.0)
                t = act(F1[:, :, :], F1[:, :, :], ACT.Ln, t, bias=1.0)
                yield
                t = stt(F2[:, :, :], z, 0.0, F1[:, :, :], ALU.max, ALU.add, t, f_free["F2"])
                for c in (0, S):
                    d = F2[:, :, c:c + P]
                    t = tt(d, d, bc(C["mask"]), ALU.mult, t)
                yield
                yield
                PE.wait(t)
                for j in range(2):
                    b = 6 + j
                    mm(ps[:, b, 0:384], C["tri"], F2[:, j, :])
                    mm(ps[:, b, P:S], C["negones"], F2[:, j, S:384])
                    for c in (0, S):
                        t = mm(ps[:, b, c:c + P], identb[:, :], negb[0][:, :], inc=(j == 1 and c == S))
                f_free["F2"] = t
                t = act(F1[:, :, :], z, ACT.Exp, t)
                yield
                yield
                t = pv(slot, i0, 2, t, toks[:-1])
                yield
                while not toks[-1]:
                    yield
                gate_out(slot, i0, h0, t, toks)
                yield

            def softmax(b0, n, scale, t, lam=None):
                V(lambda e: e.tensor_reduce(SM[:, 0:n], ps[:, b0:b0 + n, 0:P], AX.X, ALU.max), t, f_free["SM"])
                t = V(lambda e: e.tensor_reduce(SM[:, 2:2 + n], ps[:, b0:b0 + n, P:384], AX.X, ALU.max))
                t = ts(SM[:, 4:8], SM[:, 0:4], -scale, None, ALU.mult, None, t)
                for j in range(n):
                    for q in range(2):
                        c0, c1 = (0, P) if q == 0 else (P, 384)
                        cc = 2 * q + j
                        tn = A(lambda e, j=j, c0=c0, c1=c1, cc=cc: e.activation(
                            F2[:, j, c0:c1], ps[:, b0 + j, c0:c1], ACT.Exp, bias=SM[:, 4 + cc:5 + cc],
                            scale=scale, accum_out=SM[:, 8 + cc:9 + cc]), t, f_free["F2"])
                t = V(lambda e: e.reciprocal(SM[:, 12:16], SM[:, 8:12]), tn)
                return t

            f_free["SM"] = None

            def turn(j, t):
                PE.wait(t)
                tr(ps[:, 6 + j, 0:P], F2[:, j, 0:P])
                tr(ps[:, 6 + j, P:S], F2[:, j, P:S])
                return tr(ps[:, 6 + j, S:384], F2[:, j, S:384], inc=True)

            def attn_b(slot, h0, i0, toks, kr_tok):
                PE.wait(bank_free[6], bank_free[7], toks[0:4], kr_tok)
                for j in range(2):
                    b, i = 6 + j, i0 + j
                    q, k = qT[slot][:, i, :], kT[slot][:, i, :]
                    r0 = 64 * (i % 2)
                    qr, kr = qR[slot][r0:r0 + 64, i // 2, :], KR[r0:r0 + 64, :]
                    mm(ps[:, b, 0:P], q[:, 0:P], k[:, 0:P], True)
                    mm(ps[:, b, P:384], q[:, P:S], k)
                    mm(ps[:, b, 0:P], qr[:, 0:P], kr[:, 0:P])
                    mm(ps[:, b, P:384], qr[:, P:S], kr)
                    mm(ps[:, b, 0:P], identb[:, :], negb[1][:, :])
                    t = mm(ps[:, b, S:384], identb[:, :], negb[1][:, :], inc=(j == 1))
                yield
                t = softmax(6, 2, 192 ** -0.5, t)
                for j in range(2):
                    for q in range(2):
                        c0, c1 = (0, P) if q == 0 else (P, 384)
                        cc = 12 + 2 * q + j
                        t = ts(F2[:, j, c0:c1], F2[:, j, c0:c1], SM[:, cc:cc + 1], None, ALU.mult, None, t)
                yield
                yield
                turn(0, t)
                t = turn(1, t)
                f_free["F2"] = t
                t = act(F1[:, :, :], ps[:, 6:8, 0:384], ACT.Copy, t, f_free["F1"])
                yield
                t = pv(slot, i0, 2, t, toks[:-1])
                while not toks[-1]:
                    yield
                gate_out(slot, i0, h0, t, toks)
                yield

            def attn_c(slot, h, i, toks, rt_tok):
                PE.wait(bank_free[6], bank_free[7], toks, rt_tok)
                for j in range(2):
                    b, r0 = 6 + j, 64 * j
                    q, k = qT[slot][r0:r0 + 64, i, :], kT[slot][r0:r0 + 64, i, :]
                    mm(ps[:, b, 0:P], q[:, 0:P], k[:, 0:P], True)
                    mm(ps[:, b, P:384], q[:, P:S], k)
                    mm(ps[:, b, 0:P], C["flip"], RT[:, h, P:S])
                    t = mm(ps[:, b, P:384], C["flip"], RT[:, h, :], inc=(j == 1))
                yield
                t = softmax(6, 2, 1.0, t)
                t2 = ts(SM[:, 0:2], SM[:, 13:16:2], NLAM[:, 0:1], None, ALU.mult, None, t)
                t2 = ts(SM[:, 2:4], SM[:, 12:16:2], NLAM[:, 1:2], None, ALU.mult, None, t2)
                for q in range(2):
                    c0, c1 = (0, P) if q == 0 else (P, 384)
                    t = ts(F2[:, 0, c0:c1], F2[:, 0, c0:c1], SM[:, 2 + q:3 + q], None, ALU.mult,
                           None, t2)
                for q in range(2):
                    c0, c1 = (0, P) if q == 0 else (P, 384)
                    t = stt(F2[:, 0, c0:c1], F2[:, 1, c0:c1], SM[:, q:q + 1], F2[:, 0, c0:c1],
                            ALU.mult, ALU.add, t)
                yield
                yield
                t = turn(0, t)
                f_free["F2"] = t
                t = act(F1[:, 0, :], ps[:, 6, 0:384], ACT.Copy, t, f_free["F1"])
                yield
                t = pv(slot, i, 1, t, toks)
                av, sq, vv, ww = F2[:, 1, 0:S], F2[:, 0, 0:S], F1[:, 0, 0:S], F1[:, 1, 0:S]
                t = V(lambda e: e.tensor_copy(av, ps[:, 6, 0:S]), t)
                release(6, t, 1)
                t = tt(sq, av, av, ALU.mult, t)
                yield
                t = mm(ps[:, 7, 0:S], C["ones"], sq, True, t, inc=True)
                yield
                t = ts(vv, ps[:, 7, 0:S], 1.0 / P, NLAM[:, 2:3], ALU.mult, ALU.add, t)
                release(7, t, 1)
                t = ts(vv, vv, 2.0 ** -63, None, ALU.max, None, t)
                t = rsqrt(sq, vv, ww, t)
                s_ = gcol["sub"]
                t = stt(av, av, GAIN[:, s_:s_ + 1], sq, ALU.mult, ALU.mult, t)
                th = act(O[:, h, 0:S], av, ACT.Copy, t)
                t = tt(O[:, h, S:2 * S], av, O[:, h, 0:S].bitcast(F32), ALU.subtract, th)
                f_free["F1"] = f_free["F2"] = t
                o_tok[h] = t
                yield

            def proj(src, c0, xs, xt, dst, nk=KD, scale=1.0, natural=False, free=None, wk=2, view=None, nt=4,
                     r=None, silu=False):
                toks = dense(src, c0, nt, list(range(nk)), xs, xt, natural=natural, view=view, per=wk)
                if natural:
                    b, t = toks[0]
                    if r is None:
                        t = act(dst, ps[:, b:b + 2, :], ACT.Copy, t, free)
                    else:
                        for j in range(2):
                            t = act(dst[:, j, :], ps[:, b + j, :], ACT.Copy, t, need(r, 0), free,
                                    scale=RC[:, j:j + 1])
                    release(b, t)
                    return t
                return finish(toks, dst, scale, free, r, silu)

            def scaled(toks, dst, scale, r):
                ds = [dst[:, 2 * n_:2 * n_ + 2, :] for n_ in range(len(toks))]
                return [stt(d, d, scale, bc(RSX[:, :]), ALU.mult, ALU.mult, need(r, 0), t)
                        for d, t in zip(ds, toks)]

            def finish(toks, dst, scale=1.0, free=None, r=None, silu=False):
                ds = [dst[:, 2 * n_:2 * n_ + 2, :] for n_ in range(len(toks))]
                outs = [sum_pair(d, b, t, free) for d, (b, t) in zip(ds, toks)]
                if r is not None:
                    outs = scaled(outs, dst, scale, r)
                if silu:
                    outs = [act(d, d, ACT.Silu, t) for d, t in zip(ds, outs)]
                return outs

            tmpg_free = [None, None]

            def chain(*stages):
                def gen():
                    for f in stages:
                        f()
                        yield
                    chains[0] -= 1
                chains[0] += 1
                fg.append(gen())

            def summed(toks, r=None):
                while chains[0]:
                    step(fg)
                outs = []
                for i, (b, t) in enumerate(toks):
                    tm = TMPG[i][:, :, :]
                    outs.append((i, tm, sum_pair(tm, b, t, tmpg_free[i])))
                if r is not None:
                    outs = [(i, tm, stt(tm, tm, 1.0, bc(RSX[:, :]), ALU.mult, ALU.mult, need(r, 0), t))
                            for i, tm, t in outs]
                return outs

            def out_proj(src, kts, xs, xt, dst, first=True, last=True, free=None, each=None, gain=None):
                for m in range(4):
                    toks = dense(src, 512 * m, 4, kts, xs, xt)
                    if first:
                        outs = finish(toks, dst[:, 4 * m:4 * m + 4, :], free=free)
                    else:
                        outs = []
                        for n_, (i, tm, t) in enumerate(summed(toks)):
                            d = dst[:, 4 * m + 2 * n_:4 * m + 2 * n_ + 2, :]
                            tmpg_free[i] = t = tt(d, d, tm, ALU.add, t)
                            outs.append(t)
                    if last:
                        sqs = [sq_add(dst[:, 4 * m + 2 * n_:4 * m + 2 * n_ + 2, :], t) for n_, t in enumerate(outs)]
                        if gain is not None:
                            for c in range(4 * m, 4 * m + 4):
                                t_out[c] = act(dst[:, c, :], dst[:, c, :], ACT.Copy, sqs,
                                               scale=GAIN[:, gain + c:gain + c + 1])
                    if each:
                        each(m, outs)

            t_out = {}

            def residual(src, r, after):
                for c in range(0, KD, 2):
                    i, tm = tmp()
                    t = tt(tm[:, :, :], src[:, c:c + 2, :], bc(RS[:, :]), ALU.mult, r, tmp_free[i], t_out[c + 1])
                    t = tt(xT[:, c:c + 2, :], xT[:, c:c + 2, :], tm[:, :, :], ALU.add, t, st.get("xr"))
                    tmp_free[i] = t
                    rest_ = after(c, t)
                    if c:
                        rest()
                    rest = rest_
                    yield
                rest()
                yield

            def mixer_tail(l, w_out, wpp, wpg, then):
                out_proj(w_out, list(range(KD)), OB[0], lambda n: need(o_tok, n), T, free=[t_v_last[0]],
                         gain=gcol[f"post{l}"])
                pp_tok, x_tok = [], {}
                o_dead = (s_pe, PE.n)

                def pp(m, banks=None):
                    toks = dense(wpp, 512 * m, 4, [0, 1], CQ, lambda n: need(late, "p")[1], banks=banks)
                    pp_tok.extend(finish(toks, PP[:, 4 * m:4 * m + 4, :], free=slot_pe[1]))

                def split_again(c, t):
                    th = act(O[:, c:c + 2, 0:S], xT[:, c:c + 2, :], ACT.Copy, t, o_dead)

                    def low():
                        x_tok[c] = x_tok[c + 1] = tt(O[:, c:c + 2, S:2 * S], xT[:, c:c + 2, :],
                                                     O[:, c:c + 2, 0:S].bitcast(F32), ALU.subtract, th)
                    return low

                pp(0)
                r = rstd_now(D, 1e-6)
                pp(1)
                at_once(fg, residual(T, r, split_again), 1)
                pp(2)
                b = take(2)
                pp(3, [b, b + 1, 6, 7])
                h_tok = {}
                for m in range(4):
                    toks = dense(wpg, 512 * m, 4, list(range(KD)), O, lambda n: need(x_tok, n))
                    outs = summed(toks)
                    outs = [(i, tm, act(tm, tm, ACT.Sigmoid, t)) for i, tm, t in outs]
                    cs = [4 * m, 4 * m + 2]
                    done = {}

                    def update(cs=cs, outs=outs, done=done):
                        ts_ = [tt(tm, tm, PP[:, c:c + 2, :], ALU.mult, t, pp_tok[c // 2])
                               for c, (i, tm, t) in zip(cs, outs)]
                        for c, t, (i, tm, _) in zip(cs, ts_, outs):
                            done[c] = tmpg_free[i] = tt(xT[:, c:c + 2, :], xT[:, c:c + 2, :], tm, ALU.add, t)

                    def next_h(n_, cs=cs, done=done):
                        c = cs[n_]
                        low = then(c, h_tok, done[c], o_dead)
                        sq_add(xT[:, c:c + 2, :], done[c], defer=True)
                        low()
                        flush()
                        st["xr"] = st["acc"]
                    chain(update, lambda f=next_h: f(0), lambda f=next_h: f(1))
                return h_tok, (s_pe, PE.n)

            t_v_last = [None]
            w = a["w_in_a"][0]
            th_ = lambda n: need(t_h, n)
            qs = 128 ** -0.5
            for j in range(4):
                s = j % 2
                if j >= 2:
                    need(o_tok, 4 * (j - 2) + 3)
                fr = [slot_pe[s]]
                if j == 1:
                    need(late, "t")
                    fr = [late["t"], late["bv"]]
                tq = proj(w, 512 * j, H, th_, qT[s], scale=qs, free=fr, r=r_a if j else None)
                tk = proj(w, D + 512 * j, H, th_, kT[s], free=fr, r=r_a if j else None)
                tv = proj(w, 2 * D + 512 * j, H, th_, Vn[s][:, :, :], natural=True, free=fr, r=r_a)
                if j == 0:
                    tq, tk = scaled(tq, qT[0], qs, r_a), scaled(tk, kT[0], 1.0, r_a)
                tg = []
                for i0 in (0, 2):
                    bg.append(attn_a(s, 4 * j + i0, i0, [tq, tk, tv, tg]))
                tg += proj(w, 3 * D + 512 * j, H, th_, gT[s], free=fr, r=r_a, silu=True)
            h_free = (s_pe, PE.n)
            pn_free = need(late, "p")[0]
            t_kv, dead = mixer_tail(0, a["w_out_a"][0], a["w_ple_proj"][0], a["w_ple_gate"][0],
                                    lambda c, toks, t, w_: gained(c, gcol["kv"], H, toks, t, h_free, defer=True))
            t_p1 = load(PN[:, :, :], a["p"][1, 0].rearrange("(t p) d -> p t d", p=P), SP, pn_free)
            r_b, t_hb, kr = {}, {}, {}
            bg.append(later(1, rstd(D, 1e-6, RSX, r_b, True)))

            def make_hb():
                for c in range(0, KD, 2):
                    gained(c, gcol["pre1"], O, t_hb, None, dead)
                    yield
            fg.append(make_hb())
            wd = a["w_dkv"]

            def latent(src, c0, xs, xt, gname, dst, cqd, raw, free=None):
                outs = proj(src, c0, xs, xt, raw, r=r_b, free=free)
                need(done_l, "")
                done_l.clear()
                for n_, t in enumerate(outs):
                    sq_add(raw[:, 2 * n_:2 * n_ + 2, :], t)

                def norm():
                    d = {}
                    yield from later(2, rstd(512, 1e-6, RS, d))
                    done_l[""] = True
                    yield
                    yield from norm_to(raw, gcol[gname], dst, 4, d[0], cqd)
                return norm()

            def rope(xs, t, res):
                yield
                PE.wait(bank_free[7], t)
                for n_, x in enumerate(xs):
                    e_ = mm(ps[:, 7, n_ * S:(n_ + 1) * S], C["perm"], x, n_ == 0, inc=True)
                yield
                i, tm = tmp()
                for n_, x in enumerate(xs):
                    t = tt(tm[:, n_, :], ps[:, 7, n_ * S:(n_ + 1) * S], C["sin"], ALU.mult, e_, tmp_free[i])
                bank_free[7] = t
                for x in xs:
                    tc_ = tt(x, x, C["cos"], ALU.mult)
                for n_, x in enumerate(xs):
                    t = tt(x, x, tm[:, n_, :], ALU.add, t, tc_)
                tmp_free[i] = t
                res[0] = t
                yield

            t_ckv, t_cq, done_l = {}, {}, {"": True}
            bg.append(latent(wd, 0, H, lambda n: need(t_kv, n), "ckv", CKV, t_ckv, RAWL[0]))

            def view(j, k):
                if j:
                    return []
                src = wd[k * P:(k + 8) * P, 512:576].rearrange("(a p) b -> p a b", p=P)
                return [(r0, None, src) for r0 in (0, 64)]
            [(b, t)] = dense(None, 0, 1, list(range(KD)), H, lambda n: need(t_kv, n), per=8, view=view)
            hkv_dead = (s_pe, PE.n)
            t = sum_pair(KR[:, :].unsqueeze(1), b, t, n=1)
            t = tt(KR[:, :], KR[:, :], RSX[:, :], ALU.mult, t)
            bg.append(rope([KR[:, :]], t, kr))
            bg.append(latent(a["w_in_b"][0], 0, O, lambda n: need(t_hb, n), "cq", CQ, t_cq, RAWL[1],
                             t_kv[KD - 1]))
            w_uq = a["w_uq"][0].rearrange("r (h e) -> r h e", e=192)
            o_tok.clear()
            OB[0], o_war[0] = H, hkv_dead
            for j in range(4):
                s = j % 2
                if j >= 2:
                    need(o_tok, 4 * (j - 2) + 3)
                fr = [slot_pe[s]]
                tk = proj(a["w_uk"], 512 * j, CKV, lambda n: need(t_ckv, n), kT[s], nk=4, free=fr)
                tv = proj(a["w_uv"], 512 * j, CKV, lambda n: t_ckv[n], Vn[s][:, :, :], nk=4, natural=True,
                          free=fr)
                if s == 1 and j == 1:
                    need(t_cq, 3)
                    fr.append(t_cq[3])

                def group_g():
                    return proj(a["w_in_b"][0], 512 + 512 * j, O, lambda n: need(t_hb, n), gT[s],
                                free=fr, r=r_b, silu=True)
                tg = group_g() if j == 0 else []
                vq = lambda jj, k, j=j: [(jj * 512, 512, w_uq[k * P:(k + 1) * P, 4 * j:4 * j + 4, 0:128])]
                tq = proj(None, 0, CQ, lambda n: need(t_cq, n), qT[s], nk=4, free=fr, view=vq)
                vr = lambda jj, k, j=j: [(jj * 256, 256, w_uq[k * P:(k + 1) * P, 4 * j:4 * j + 4, 128:192])]
                tr_ = proj(None, 0, CQ, lambda n: t_cq[n], qR[s], nk=4, free=fr, view=vr, wk=4, nt=2)
                qr = {}
                bg.append(rope([qR[s][:, i, :] for i in range(2)], tr_, qr))
                for i0 in (0, 2):
                    def both(i0=i0, s=s, j=j, toks=[tk, tq, tr_, tv, tg], qr=qr):
                        yield from attn_b(s, 4 * j + i0, i0, toks, [kr[0], qr[0]])
                    bg.append(both())
                if j > 0:
                    tg += group_g()
            cq_dead = (s_pe, PE.n)
            late.pop("p")

            def p_again():
                late["p"] = p_split(t_p1, cq_dead)
                yield
            bg.append(p_again())
            t_h2, dead = mixer_tail(1, a["w_out_b"][0], a["w_ple_proj"][1], a["w_ple_gate"][1],
                                    lambda c, toks, t, w_: gained(c, gcol["mixpre"], H, toks, t, w_, defer=True))
            r_c = {}
            bg.append(later(2, rstd(D, 1e-6, RSX, r_c, True)))
            i = small[0]
            small[0] += 1
            GP.wait(late["bv"], late["p"][1], dead)
            for h in range(8):
                src = bass.AP(bvd.tensor, h * 384, [[1, P], [1, S]])
                rt_tok = GP.dma(lambda e, h=h, src=src: e.dma_start(RT[:, h, :], src), s_in[i], 16 * (h + 1))
            th2 = lambda n: need(t_h2, n)
            w = a["w_in_2"][0]
            o_tok.clear()
            OB[0], o_war[0] = O, dead
            for j in range(2):
                fr = [slot_pe[j], st["xr"]]
                tq = proj(w, 512 * j, H, th2, qT[j], scale=0.125, free=fr, r=r_c)
                tk = proj(w, 1024 + 512 * j, H, th2, kT[j], free=fr, r=r_c)
                tv = proj(w, 2048 + 512 * j, H, th2, Vn[j][:, :, :], natural=True, free=fr, r=r_c)
                for i in range(4):
                    bg.append(attn_c(j, 4 * j + i, i, [tq, tk, tv], rt_tok))
            for m in range(2):
                tg_ = proj(w, 4096 + 512 * m, H, th2, GC, r=r_c)
                outs = summed(dense(w, 5120 + 512 * m, 4, list(range(KD)), H, th2), r_c)
                t_u, t_y = [], []
                for n_, (i, tm, t) in enumerate(outs):
                    g = GC[:, 2 * n_:2 * n_ + 2, :]
                    tmpg_free[i] = t = tt(g, g, tm, ALU.mult, t, tg_)
                    t_u.append(t)

                def fir(n_, m=m, t_u=t_u, t_y=t_y):
                    cws = [[GAIN[:, gcol[f"cw{q}"] + ch:gcol[f"cw{q}"] + ch + 1] for q in range(3)]
                           for ch in (4 * m + 2 * n_, 4 * m + 2 * n_ + 1)]
                    uy = [(GC[:, 2 * n_ + jj, :], CT[m][:, 2 * n_ + jj, :]) for jj in range(2)]
                    tk_ = [ts(y, u, cw[2], None, ALU.mult, None, t_u[n_], slot_pe[0] if m else None)
                           for (u, y), cw in zip(uy, cws)]
                    tk_ = [stt(y[:, 1:S], u[:, 0:S - 1], cw[1], y[:, 1:S], ALU.mult, ALU.add, t)
                           for t, (u, y), cw in zip(tk_, uy, cws)]
                    tk_ = [stt(y[:, 2:S], u[:, 0:S - 2], cw[0], y[:, 2:S], ALU.mult, ALU.add, t)
                           for t, (u, y), cw in zip(tk_, uy, cws)]
                    t_y.append(tk_[1])
                if m == 1:
                    need(o_tok, 3)
                chain(lambda f=fir: f(0), lambda f=fir: f(1))
                toks = dense(w, 3072 + 512 * m, 4, list(range(KD)), H, th2)
                outs = summed(toks, r_c)

                def conv(n_, m=m, outs=outs, t_y=t_y):
                    i, tm, t = outs[n_]
                    c2 = CT[m][:, 2 * n_:2 * n_ + 2, :]
                    tmpg_free[i] = t = tt(c2, c2, tm, ALU.mult, t, t_y[n_])
                    sq_add(c2, t)
                if m == 0:
                    chain(lambda f=conv: f(0), lambda f=conv: f(1))
                else:
                    conv(0)
                    conv(1)
            h2_dead = (s_pe, PE.n)

            def conv_norm():
                d = {}
                yield from later(1, rstd(1024, 1e-6, RS, d, ring_bank=True))
                cn = gcol["cn"]
                for c in range(0, 8, 2):
                    i, tm = tmp()
                    for j in range(2):
                        t = stt(tm[:, j, :], CT[c // 4][:, c % 4 + j, :], GAIN[:, cn + c + j:cn + c + j + 1], RS[:, :],
                                ALU.mult, ALU.mult, d[0], tmp_free[i])
                    t = split_x(tm[:, :, :], O, 8 + c, 2, t)
                    tmp_free[i] = t
                    o_tok[8 + c] = o_tok[9 + c] = t
                    yield
            fg.append(conv_norm())
            out_proj(a["w_out_2"][0], list(range(KD)), O, lambda n: need(o_tok, n), T, gain=gcol["mixpost"])
            r = rstd_now(D, 1e-6)
            t_h3, r_d = {}, {}

            def h3(c, t):
                low = gained(c, gcol["ffnpre"], H, t_h3, t, h2_dead, defer=True)
                add = sq_pe(xT[:, c:c + 2, :], t, c // 2)

                def rest():
                    low()
                    add()
                    if c == KD - 2:
                        st["xr"] = st["bank"]
                        bg.append(later(1, rstd(D, 1e-6, RSX, r_d)))
                return rest
            at_once(fg, residual(T, r, h3), 1)
            th3 = lambda n: need(t_h3, n)
            wg, wu, wdn = a["w_gate_2"][0], a["w_up_2"][0], a["w_down_2"][0]
            acts_free = (s_pe, PE.n)
            for part, (f0, f1) in enumerate(((0, 6), (6, 11))):
                a_tok = {}
                for f in range(f0, f1):
                    toks = dense(wg, 512 * f, 4, list(range(KD)), H, th3)
                    need(t_h3, KD - 1)
                    sg = finish(toks, SG, r=r_d, silu=True)
                    toks = dense(wu, 512 * f, 4, list(range(KD)), H, th3)
                    outs = summed(toks, r_d)

                    def up(n_, outs=outs, sg=sg, f=f, f0=f0, war=acts_free, a_tok=a_tok):
                        i, tm, t = outs[n_]
                        t = tt(tm, tm, SG[:, 2 * n_:2 * n_ + 2, :], ALU.mult, t, sg[n_])
                        k = 4 * (f - f0) + 2 * n_
                        tmpg_free[i] = a_tok[k] = a_tok[k + 1] = split_x(tm, ACTS, k, 2, t, war)
                    chain(lambda f=up: f(0), lambda f=up: f(1))
                acts = lambda n, a_tok=a_tok: need(a_tok, n)
                if part == 0:
                    out_proj(wdn, list(range(4 * f0, 4 * f1)), ACTS, acts, T2, last=False)
                    acts_free = (s_pe, PE.n)
            h3_dead = (s_pe, PE.n)
            x_done = st["xr"]

            def to_rows(src, m, dst, dep):
                PE.wait(bank_free[6], bank_free[7], dep)
                for t in range(2):
                    for j in range(4):
                        e_ = tr(ps[:, 6 + t, j * P:(j + 1) * P], src[:, 4 * m + j, t * P:(t + 1) * P],
                                inc=(t == 1 and j == 3))
                yield
                t_ = act(dst[:, :, 512 * m:512 * m + 512], ps[:, 6:8, :], ACT.Copy, e_, h3_dead)
                release(6, t_)
                rows_tok[0] = t_

            rows_tok = {}

            def rows(m, toks):
                def gen():
                    for j in range(4):
                        c = 4 * m + j
                        g = GAIN[:, gcol["ffnpost"] + c:gcol["ffnpost"] + c + 1]
                        t = act(T2[:, c, :], T2[:, c, :], ACT.Copy, toks, st["acc"], scale=g)
                    yield
                    yield from to_rows(T2, m, TNAT, t)
                    if m < 3:
                        yield
                        yield from to_rows(xT, m, XNAT, x_done)
                        yield
                        if m == 2:
                            yield from to_rows(xT, 3, XNAT, x_done)
                bg.append(gen())
            out_proj(wdn, list(range(24, 44)), ACTS, acts, T2, first=False, each=rows)
            sq_tok = st["acc"]
            for t in range(2):
                for j in range(2):
                    e_ = mm(ps[:, 5, t:t + 1], ACC[:, j, t * P:(t + 1) * P], C["ones"][:, 0:1],
                            t == 0 and j == 0, sq_tok, bank_free[5], inc=(t == 1 and j == 1))
            t = ts(RV[:, 0:2], ps[:, 5, 0:2], 1.0 / D, 1e-6, ALU.mult, ALU.add, e_)
            t = rsqrt(RC[:, :], RV[:, 0:2], RW[:, 0:2], t)
            drain()
            y = out.rearrange("a (t p) d -> p (a t) d", p=P)
            nout = 0
            for n_ in (0, 1):
                for t_ in range(2):
                    d = TNAT[:, t_, 1024 * n_:1024 * n_ + 1024]
                    t = stt(d, d, RC[:, t_:t_ + 1], XNAT[:, t_, 1024 * n_:1024 * n_ + 1024], ALU.mult, ALU.add,
                            t, rows_tok[0])
                    nout += 16
                    SP.dma(lambda e, d=d, t_=t_, n_=n_: e.dma_start(y[:, t_, 1024 * n_:1024 * n_ + 1024], d),
                           s_out, nout, t)
            SP.wait(late["bv"], (s_out, nout))
            return chunks, PE, AC, DV, SP, GP

        chunks, *_ = program([])
        _, PE, AC, DV, SP, GP = program(chunks)
        block = ctx.enter_context(nc.Block())

        @block.tensor
        def _(e):
            PE.play(e)

        @block.vector
        def _(e):
            DV.play(e)

        @block.scalar
        def _(e):
            AC.play(e)

        @block.gpsimd
        def _(e):
            GP.play(e)

        @block.sync
        def _(e):
            SP.play(e)


_INS = ["x", "p", "w_in_a", "w_out_a", "w_in_b", "w_uq", "w_out_b", "w_dkv", "w_uk", "w_uv", "w_ple_proj",
        "w_ple_gate", "w_in_2", "w_out_2", "rel_bias_2", "w_gate_2", "w_up_2", "w_down_2"]


def constants():
    f = np.float32
    i = np.arange(P)
    t = {}
    t["ident"] = np.eye(P, dtype=f)
    t["flip"] = np.eye(P, dtype=f)[::-1]
    t["tri"] = -(i[:, None] >= i[None, :]).astype(f)
    t["ones"] = np.ones((P, P), f)
    perm = np.zeros((P, P), f)
    perm[i ^ 32, i] = 1.0
    t["perm"] = perm
    t["mask"] = (i[:, None] < i[None, :]).astype(f)
    t["negA"] = np.where(i[:, None] >= i[None, :], f(-1e30), f(0))
    t["negB"] = np.where((i[:, None] < 64) & (i[None, :] >= 64), f(-1e30), f(0))
    inv = (f(1.0) / (f(10000.0) ** (np.arange(0, 64, 2, dtype=f) / f(64)))).astype(f)
    ang = np.arange(S, dtype=f)[None, :] * inv[i % 32][:, None]
    t["cos"] = np.cos(ang).astype(f)
    t["sin"] = (np.sin(ang) * np.where(i % 64 < 32, -1.0, 1.0)[:, None]).astype(f)
    t["negones"] = -t["ones"]
    cst = np.concatenate([t[n].astype(f) for n in CONST + ["negA", "negB"]], axis=1)
    d = 255 - np.arange(384)
    n = np.maximum(d, 0)
    nf = np.maximum(n, 16).astype(f)
    large = 16 + (np.log(nf / f(16)) / f(math.log(8.0)) * f(16)).astype(np.int32)
    large = np.minimum(large, 31)
    bucket = np.where(n < 16, n, large)
    oh = np.zeros((33, 384), f)
    oh[bucket, np.arange(384)] = 1.0
    oh[32] = np.where(d < 0, f(-1e30), f(0))
    return np.ascontiguousarray(cst), oh


def kernel(**inputs):
    import concourse.bacc as _bacc
    from concourse.bass_utils import run_bass_kernel_spmd as _run

    nc = _bacc.Bacc("TRN2", target_bir_lowering=False, num_devices=1)
    arrays, aps = {}, {}
    for name in _INS:
        v = np.ascontiguousarray(inputs[name])
        arrays[f"in_{name}"] = v
        aps[name] = nc.dram_tensor(f"in_{name}", v.shape, mybir.dt.from_np(v.dtype), kind="ExternalInput").ap()
    cst, oh = constants()
    arrays["cst"], arrays["oh"] = cst, oh
    c_ap = nc.dram_tensor("cst", cst.shape, F32, kind="ExternalInput").ap()
    o_ap = nc.dram_tensor("oh", oh.shape, F32, kind="ExternalInput").ap()
    rows = [inputs["norm_pre"][0], inputs["norm_pre"][1], inputs["norm_mix_pre_2"], inputs["norm_post"][0],
            inputs["norm_post"][1], inputs["kv_norm"], inputs["norm_mix_post_2"], inputs["norm_ffn_pre_2"],
            inputs["norm_ffn_post_2"], inputs["kv_latent_norm"], inputs["q_latent_norm"], inputs["conv_w_2"],
            inputs["conv_norm_gain_2"], inputs["subln_gain_2"]]
    arrays["gains"] = np.concatenate([np.asarray(v).reshape(-1, P) for v in rows])
    arrays["lams"] = np.stack([np.asarray(inputs[f"lambda_{n}_2"]) for n in ("q1", "k1", "q2", "k2")], 1)
    g_ap = nc.dram_tensor("gains", arrays["gains"].shape, F32, kind="ExternalInput").ap()
    l_ap = nc.dram_tensor("lams", arrays["lams"].shape, F32, kind="ExternalInput").ap()
    y = nc.dram_tensor("out", (1, S, D), F32, kind="ExternalOutput").ap()
    build(nc, aps, c_ap, o_ap, g_ap, l_ap, y)
    r = _run(nc, [arrays], core_ids=[0])
    return r.results[0]["out"]
```
